# Optimizing a Trainium2 kernel written in Bass

```python
import jax
import jax.numpy as jnp
from jax import lax
import numpy as np

D_MODEL = 1024
BATCH = 1
SEQ = 256
DEPTH = 2
DEC_BATCH = 8
DEC_SEQ = 4
PAST_LEN = 2048
PAGE_SIZE = 128

MIX_WIDTH = D_MODEL
CONV_WIDTH = MIX_WIDTH // 2
CONV_K = 3
DN_HEADS = 4
DN_HEAD_DIM = (MIX_WIDTH - CONV_WIDTH) // DN_HEADS
DN_WIDTH = DN_HEADS * DN_HEAD_DIM
DN_CONV_K = 4
DN_CHUNK = 64
D_FF = 2816
N_EXPERTS = 8
TOP_K = 2
D_EXPERT = D_FF // 2
N_DENSE = (DEPTH + 1) // 2
N_MOE = DEPTH // 2
DEEPNORM_ALPHA = (2.0 * DEPTH) ** 0.25
DEEPNORM_BETA = (8.0 * DEPTH) ** -0.25
LN_EPS = 1e-5
RMS_EPS = 1e-6

OFF_CB = 0
OFF_CC = OFF_CB + CONV_WIDTH
OFF_CH = OFF_CC + CONV_WIDTH
OFF_QKV = OFF_CH + CONV_WIDTH
OFF_Z = OFF_QKV + 3 * DN_WIDTH
OFF_BETA = OFF_Z + DN_WIDTH
OFF_A = OFF_BETA + DN_HEADS
P_TOTAL = OFF_A + DN_HEADS

kernel_name = 'hymba_conv_gdn_deepnorm_adaln_step'

F32 = jnp.float32

def layer_norm(x, g, b):
    xf = x.astype(F32)
    mu = jnp.mean(xf, -1, keepdims=True)
    xc = xf - mu
    var = jnp.mean(xc * xc, -1, keepdims=True)
    return (xc * lax.rsqrt(var + LN_EPS) * g.astype(F32) + b.astype(F32)).astype(x.dtype)

def l2norm(x):
    return x * lax.rsqrt(jnp.sum(x * x, -1, keepdims=True) + RMS_EPS)

def causal_dwconv(u, buf, w):
    k = w.shape[0]
    t = u.shape[1]
    ext = jnp.concatenate([buf.astype(u.dtype), u], axis=1)
    y = ext[:, 0:t] * w[0]
    for i in range(1, k):
        y = y + ext[:, i:i + t] * w[i]
    return y, ext[:, ext.shape[1] - (k - 1):]

def gated_delta_rule(q, k, v, g, beta, s0):
    bsz, t, h, dk = q.shape
    dv = v.shape[-1]
    c = min(DN_CHUNK, t)
    n = -(-t // c)
    pad = n * c - t
    if pad:
        pw = ((0, 0), (0, pad), (0, 0), (0, 0))
        q = jnp.pad(q, pw)
        k = jnp.pad(k, pw)
        v = jnp.pad(v, pw)
        g = jnp.pad(g, pw[:3])
        beta = jnp.pad(beta, pw[:3])

    def blk(a):
        a = a.reshape((bsz, n, c, h) + a.shape[3:])
        return jnp.moveaxis(a, (1, 3), (0, 2))

    qb, kb, vb, gb, bb = blk(q), blk(k), blk(v), blk(g), blk(beta)
    gc = jnp.cumsum(gb, axis=-1)
    causal = jnp.tril(jnp.ones((c, c), dtype=bool))
    strict = jnp.tril(jnp.ones((c, c), dtype=bool), -1)
    gamma = jnp.exp(jnp.where(causal, gc[..., :, None] - gc[..., None, :], -jnp.inf))
    kbeta = kb * bb[..., None]
    m = jnp.where(strict, jnp.einsum('nbhcd,nbhsd->nbhcs', kbeta, kb) * gamma, 0.0)
    a_mat = jnp.eye(c, dtype=F32) + m
    rhs = jnp.concatenate([kbeta * jnp.exp(gc)[..., None], vb * bb[..., None]], axis=-1)
    sol = lax.linalg.triangular_solve(a_mat, rhs, left_side=True, lower=True, unit_diagonal=True)
    w_blk, u_blk = sol[..., :dk], sol[..., dk:]
    attn = jnp.einsum('nbhcd,nbhsd->nbhcs', qb, kb) * gamma
    q_dec = qb * jnp.exp(gc)[..., None]
    k_dec = kb * jnp.exp(gc[..., -1:] - gc)[..., None]
    last_decay = jnp.exp(gc[..., -1])

    def step(s, xs):
        w_c, u_c, q_c, a_c, k_c, d_c = xs
        v_new = u_c - jnp.einsum('bhcd,bhde->bhce', w_c, s)
        o_c = jnp.einsum('bhcd,bhde->bhce', q_c, s) + jnp.einsum('bhcs,bhse->bhce', a_c, v_new)
        s = s * d_c[..., None, None] + jnp.einsum('bhcd,bhce->bhde', k_c, v_new)
        return s, o_c

    s_fin, o = lax.scan(step, s0, (w_blk, u_blk, q_dec, attn, k_dec, last_decay))
    o = jnp.moveaxis(o, (0, 2), (1, 3)).reshape(bsz, n * c, h, dv)[:, :t]
    return o, s_fin

def mixer(u, conv_buf, dn_buf, s0, w_in, conv_w, dn_conv_w, a_log, dt_bias, dn_norm_w, w_out):
    bsz, t, _ = u.shape
    p = u @ w_in
    gate_b = p[..., OFF_CB:OFF_CC]
    gate_c = p[..., OFF_CC:OFF_CH]
    h_in = p[..., OFF_CH:OFF_QKV]
    yc, new_conv_buf = causal_dwconv(gate_c * h_in, conv_buf, conv_w)
    y_conv = gate_b * yc
    qkv, new_dn_buf = causal_dwconv(p[..., OFF_QKV:OFF_Z], dn_buf, dn_conv_w)
    qkv = jax.nn.silu(qkv.astype(F32))
    q = qkv[..., 0:DN_WIDTH].reshape(bsz, t, DN_HEADS, DN_HEAD_DIM)
    k = qkv[..., DN_WIDTH:2 * DN_WIDTH].reshape(bsz, t, DN_HEADS, DN_HEAD_DIM)
    v = qkv[..., 2 * DN_WIDTH:].reshape(bsz, t, DN_HEADS, DN_HEAD_DIM)
    q = l2norm(q) * (DN_HEAD_DIM ** -0.5)
    k = l2norm(k)
    z = p[..., OFF_Z:OFF_BETA].astype(F32)
    beta = jax.nn.sigmoid(p[..., OFF_BETA:OFF_A].astype(F32))
    g = -jnp.exp(a_log.astype(F32)) * jax.nn.softplus(p[..., OFF_A:P_TOTAL].astype(F32) + dt_bias.astype(F32))
    o, s_new = gated_delta_rule(q, k, v, g, beta, s0.astype(F32))
    o = o * lax.rsqrt(jnp.mean(o * o, -1, keepdims=True) + RMS_EPS) * dn_norm_w.astype(F32)
    o = o.reshape(bsz, t, DN_WIDTH) * jax.nn.silu(z)
    mixed = jnp.concatenate([y_conv, o.astype(u.dtype)], axis=-1)
    return mixed @ w_out, new_conv_buf, new_dn_buf, s_new

def dense_ffn(u, w_gate, w_up, w_down):
    return (jax.nn.silu(u @ w_gate) * (u @ w_up)) @ w_down

def moe_ffn(u, w_router, b_router, w_gate, w_up, w_down):
    logits = (u @ w_router).astype(F32) + b_router.astype(F32)
    probs = jax.nn.softmax(logits, axis=-1)
    top_p, top_i = lax.top_k(probs, TOP_K)
    top_p = top_p / jnp.sum(top_p, -1, keepdims=True)
    gates = jnp.sum(jax.nn.one_hot(top_i, N_EXPERTS, dtype=F32) * top_p[..., None], axis=-2)
    y = jnp.zeros(u.shape, F32)
    for e in range(N_EXPERTS):
        h = jax.nn.silu(u @ w_gate[e]) * (u @ w_up[e])
        y = y + gates[..., e:e + 1] * (h @ w_down[e]).astype(F32)
    return y.astype(u.dtype)

def trunk(x, c, conv_bufs, dn_bufs, s0s, prm):
    new_conv, new_dnc, new_s = [], [], []
    for l in range(DEPTH):
        mod = jax.nn.silu(c) @ prm['w_ada'][l] + prm['b_ada'][l]
        sh1, sc1, g1, sh2, sc2, g2 = jnp.split(mod[:, None, :], 6, axis=-1)
        u = x * (1 + sc1) + sh1
        m, cb, db, s = mixer(u, conv_bufs[l], dn_bufs[l], s0s[l], prm['w_in'][l], prm['conv_w'][l],
                             prm['dn_conv_w'][l], prm['a_log'][l], prm['dt_bias'][l],
                             prm['dn_norm_w'][l], prm['w_out'][l])
        new_conv.append(cb)
        new_dnc.append(db)
        new_s.append(s)
        x = layer_norm(DEEPNORM_ALPHA * x + (1 + g1) * m, prm['ln_g'][l, 0], prm['ln_b'][l, 0])
        u = x * (1 + sc2) + sh2
        j = l // 2
        if l % 2 == 0:
            f = dense_ffn(u, prm['w_ff_gate'][j], prm['w_ff_up'][j], prm['w_ff_down'][j])
        else:
            f = moe_ffn(u, prm['w_router'][j], prm['b_router'][j], prm['w_exp_gate'][j],
                        prm['w_exp_up'][j], prm['w_exp_down'][j])
        x = layer_norm(DEEPNORM_ALPHA * x + (1 + g2) * f, prm['ln_g'][l, 1], prm['ln_b'][l, 1])
    return x, jnp.stack(new_conv), jnp.stack(new_dnc), jnp.stack(new_s)

def setup_inputs(seed: int = 0) -> dict:
    key = jax.random.key(seed)
    ks = jax.random.split(key, 32)
    nrm = jax.random.normal
    d = D_MODEL
    dt = jnp.exp(jax.random.uniform(ks[10], (DEPTH, DN_HEADS), F32, np.log(1e-3), np.log(1e-1)))
    return {
        'x_prompt': nrm(ks[0], (BATCH, SEQ, d), F32),
        'x_sample': nrm(ks[1], (DEC_BATCH, DEC_SEQ, d), F32),
        'state_conv': nrm(ks[2], (DEPTH, DEC_BATCH, CONV_K - 1, CONV_WIDTH), F32),
        'state_dn_conv': nrm(ks[3], (DEPTH, DEC_BATCH, DN_CONV_K - 1, 3 * DN_WIDTH), F32),
        'state_dn': 0.1 * nrm(ks[4], (DEPTH, DEC_BATCH, DN_HEADS, DN_HEAD_DIM, DN_HEAD_DIM), F32),
        'c_prompt': nrm(ks[5], (BATCH, d), F32),
        'c_sample': nrm(ks[6], (DEC_BATCH, d), F32),
        'w_in': nrm(ks[7], (DEPTH, d, P_TOTAL), F32) * d ** -0.5,
        'conv_w': nrm(ks[8], (DEPTH, CONV_K, CONV_WIDTH), F32) * CONV_K ** -0.5,
        'dn_conv_w': nrm(ks[9], (DEPTH, DN_CONV_K, 3 * DN_WIDTH), F32) * DN_CONV_K ** -0.5,
        'a_log': jnp.log(jax.random.uniform(ks[11], (DEPTH, DN_HEADS), F32, 1.0, 16.0)),
        'dt_bias': dt + jnp.log(-jnp.expm1(-dt)),
        'dn_norm_w': 1.0 + 0.02 * nrm(ks[12], (DEPTH, DN_HEAD_DIM), F32),
        'w_out': nrm(ks[13], (DEPTH, MIX_WIDTH, d), F32) * MIX_WIDTH ** -0.5 * DEEPNORM_BETA,
        'w_ada': nrm(ks[14], (DEPTH, d, 6 * d), F32) * d ** -0.5 * 0.2,
        'b_ada': 0.02 * nrm(ks[15], (DEPTH, 6 * d), F32),
        'ln_g': 1.0 + 0.02 * nrm(ks[16], (DEPTH, 2, d), F32),
        'ln_b': 0.02 * nrm(ks[17], (DEPTH, 2, d), F32),
        'w_ff_gate': nrm(ks[18], (N_DENSE, d, D_FF), F32) * d ** -0.5,
        'w_ff_up': nrm(ks[19], (N_DENSE, d, D_FF), F32) * d ** -0.5,
        'w_ff_down': nrm(ks[20], (N_DENSE, D_FF, d), F32) * D_FF ** -0.5 * DEEPNORM_BETA,
        'w_router': nrm(ks[21], (N_MOE, d, N_EXPERTS), F32) * d ** -0.5,
        'b_router': 0.01 * nrm(ks[22], (N_MOE, N_EXPERTS), F32),
        'w_exp_gate': nrm(ks[23], (N_MOE, N_EXPERTS, d, D_EXPERT), F32) * d ** -0.5,
        'w_exp_up': nrm(ks[24], (N_MOE, N_EXPERTS, d, D_EXPERT), F32) * d ** -0.5,
        'w_exp_down': nrm(ks[25], (N_MOE, N_EXPERTS, D_EXPERT, d), F32) * D_EXPERT ** -0.5 * DEEPNORM_BETA,
    }

def reference(x_prompt, x_sample, state_conv, state_dn_conv, state_dn, c_prompt, c_sample,
              w_in, conv_w, dn_conv_w, a_log, dt_bias, dn_norm_w, w_out, w_ada, b_ada, ln_g, ln_b,
              w_ff_gate, w_ff_up, w_ff_down, w_router, b_router, w_exp_gate, w_exp_up, w_exp_down):
    prm = {'w_in': w_in, 'conv_w': conv_w, 'dn_conv_w': dn_conv_w, 'a_log': a_log, 'dt_bias': dt_bias,
           'dn_norm_w': dn_norm_w, 'w_out': w_out, 'w_ada': w_ada, 'b_ada': b_ada, 'ln_g': ln_g,
           'ln_b': ln_b, 'w_ff_gate': w_ff_gate, 'w_ff_up': w_ff_up, 'w_ff_down': w_ff_down,
           'w_router': w_router, 'b_router': b_router, 'w_exp_gate': w_exp_gate,
           'w_exp_up': w_exp_up, 'w_exp_down': w_exp_down}
    bp = x_prompt.shape[0]
    zc = [jnp.zeros((bp, CONV_K - 1, CONV_WIDTH), x_prompt.dtype) for _ in range(DEPTH)]
    zd = [jnp.zeros((bp, DN_CONV_K - 1, 3 * DN_WIDTH), x_prompt.dtype) for _ in range(DEPTH)]
    zs = [jnp.zeros((bp, DN_HEADS, DN_HEAD_DIM, DN_HEAD_DIM), F32) for _ in range(DEPTH)]
    y_prompt, conv_p, dnc_p, dn_p = trunk(x_prompt, c_prompt, zc, zd, zs, prm)
    y_sample, conv_s, dnc_s, dn_s = trunk(
        x_sample, c_sample,
        [state_conv[l] for l in range(DEPTH)],
        [state_dn_conv[l] for l in range(DEPTH)],
        [state_dn[l] for l in range(DEPTH)], prm)
    return (y_prompt, y_sample, conv_p, dnc_p, dn_p, conv_s, dnc_s, dn_s)


_drawn_inputs = setup_inputs


def setup_inputs(seed=0):
    import zlib

    import numpy as np

    out = dict(_drawn_inputs(seed))
    spreads = {}
    factors = {'dn_norm_w': 7.359, 'b_router': 4.078}
    for name, (base, spread) in spreads.items():
        noise = np.random.default_rng([zlib.crc32(name.encode()), seed]).standard_normal(out[name].shape)
        drawn = base * np.exp(spread * noise) if base else spread * noise
        out[name] = jnp.asarray(drawn.astype(out[name].dtype))
    for name, factor in factors.items():
        out[name] = (out[name] * factor).astype(out[name].dtype)
    return out
```

```python
from contextlib import ExitStack

import concourse.bass as bass
from concourse import mybir

F32 = mybir.dt.float32
F32R = mybir.dt.float32r
ALU = mybir.AluOpType
ACT = mybir.ActivationFunctionType
AX_X = mybir.AxisListType.X

P = 128
D = 1024
KT = D // P
NP_ = 256
NSEQ = 8
NT = 4
NS = NSEQ * NT
N = NP_ + NS
DEPTH = 2
CW = 512
CT = CW // P
H = 4
QT = 3 * H
CK, DK = 3, 4
CE = NP_ + CK - 1 + NSEQ * (NT + CK - 1)
DE = NP_ + DK - 1 + NSEQ * (NT + DK - 1)
DS0 = NP_ + DK - 1
CS0 = NP_ + CK - 1
PTOT = 3592
FF = 2816
FT = FF // P
NE = 8
DX = FF // 2
XT = DX // P
QTR = KT // 2
ALPHA = (2.0 * DEPTH) ** 0.25
LN_EPS = 1e-5
RMS_EPS = 1e-6

NU = 9
DEC = 8
C1U = [1, 3, 5, 7, 8]

BLK = 2048
RAW = 6
SPLIT = 2

W_IN = [('k', 8), ('k', 9), ('q', 6), ('q', 7), ('v', 10), ('v', 11),
        ('z', 12), ('z', 13), ('c', 2), ('h', 4), ('c', 3), ('h', 5), ('b', 0), ('b', 1)]
ADA_CB = 6 * D // 512
LEVELS = [2, 4, 8, 16, 32, 64]

GRP = {'A': (2, 3, [0, 1, 2, 3]), 'B': (6, 7, [4, 5, 6, 7]), 'C': (2, 3, [8])}

XCB = -(-DX // 256)
XUP = 2 * XCB
XD_K = [6, XT - 6]
XDB = D // 256
XB = XUP + 2 * XDB
XRAW = 5
XSPLIT = 4
TT = 96
NTT = N // TT


def steps_of():
    s = [('start',), ('params',)]
    ada = [(0, c) for c in range(ADA_CB)] + [(1, c) for c in range(ADA_CB)]
    last = []

    def more_ada(n=1):
        for _ in range(n):
            if ada:
                a = ada.pop(0)
                if last:
                    s.append(('adaT', *last.pop()))
                s.append(('ada', *a))
                last.append(a)

    def flush():
        if last:
            s.append(('adaT', *last.pop()))

    def tile(l, m, t):
        s.append(('pt', l, m, t))

    for l in range(DEPTH):
        if l == 0:
            more_ada(4)
            flush()
        s += [('u', l, 0), ('ba', l), ('st_in', l), ('ba2', l)]
        fill = [(m, t) for m in range(6, 14) for t in range(2)]

        def filler(n):
            for _ in range(n):
                if fill:
                    m, t = fill.pop(0)
                    tile(l, m, t)
                    if t == 1:
                        more_ada()
        for m in range(2):
            tile(l, m, 0)
            tile(l, m, 1)
        s.append(('conv', l, 'k'))
        for m in range(2, 4):
            tile(l, m, 0)
            tile(l, m, 1)
            more_ada(l == 0)
        s += [('ss', l, 'k'), ('conv', l, 'q')]
        for m in range(4, 6):
            tile(l, m, 0)
            tile(l, m, 1)
            more_ada(l == 0)
        s += [('ss', l, 'q'), ('conv', l, 'v'), ('gc', l)]
        filler(1)
        s.append(('st_out', l))
        filler(1)
        s.append(('tok', l))
        s.append(('att', l))
        filler(1)
        s.append(('kk', l))
        filler(1)
        s.append(('mt', l))
        filler(1)
        for lev in LEVELS:
            for k in 'XY':
                s.append((k, l, lev, 'A'))
                s.append((k, l, lev, 'B'))
                if lev == 2:
                    s.append((k, l, lev, 'C'))
                filler(1)
        s.append(('wt', l))
        filler(1)
        s.append(('c0', l))
        filler(1)
        s.append(('c1', l))
        filler(1)
        s.append(('c2', l))
        filler(99)
        s += [('su', l, h) for h in range(H)]
        s.append(('on', l))
        more_ada()
        s += [('cs_out', l), ('mix', l)]
        for m in range(4):
            for t in range(2):
                s.append(('wo', l, m, t))
            if m:
                more_ada()
        s.append(('lnm', l, 0))
        more_ada()
        s.append(('lnv', l, 0))
        more_ada(3)
        flush()
        s.append(('u', l, 1))
        s.append(('ffn', l) if l % 2 == 0 else ('moe', l))
        s += [('lnm', l, 1), ('lnv', l, 1)]
    assert not ada and not last
    s.append(('out',))
    return s


STEPS = steps_of()


OUT_BANKS = (0, 1, 2, 3, 6, 7)


def banks_of(step):
    k = step[0]
    one = lambda *b: {x: 1 for x in b}
    if k == 'start':
        return one(*range(8))
    if k == 'params':
        return one(0, 1, 2)
    if k == 'ada':
        return one(4)
    if k == 'adaT':
        return one(5)
    if k in ('ba', 'ba2'):
        return one(7)
    if k == 'st_in':
        return one(6)
    if k in ('pt', 'wo'):
        return one(step[3])
    if k in ('ss', 'gc', 'on'):
        return one(2, 3, 6, 7)
    if k == 'st_out':
        return one(2, 3, 6)
    if k == 'cs_out':
        return one(6)
    if k == 'tok':
        return {2: 2, 3: 2, 6: 1, 7: 1}
    if k == 'att':
        return one(6, 7, 2)
    if k == 'kk':
        return one(3, 6, 7)
    if k == 'mt':
        return one(2, 3, 6)
    if k == 'X':
        return one(GRP[step[3]][0])
    if k == 'Y':
        return one(*(GRP[step[3]][:2] if step[2] < 64 else GRP[step[3]][1:2]))
    if k == 'wt':
        return one(2, 3, 6)
    if k == 'c0':
        return one(7, 2, 3)
    if k == 'c1':
        return one(6, 3)
    if k == 'c2':
        return one(7, 2, 3)
    if k == 'su':
        return one(*((2, 3) if step[2] % 2 == 0 else (6, 7)))
    if k == 'lnm':
        return one(6)
    if k == 'lnv':
        return one(7)
    if k == 'out':
        return one(*OUT_BANKS)
    return {}


def positions():
    n = m = a = 0
    out = []
    for s in STEPS:
        out.append((n, m, a))
        if s[0] == 'ada':
            n, a = n + 2, a + 2
        elif s[0] in ('pt', 'wo') and s[3] == 0:
            n, m = n + 1, m + 1
        elif s[0] == 'ffn':
            n, m = n + FFN_BLOCKS, m + FFN_BLOCKS
    return out


UP_CB = FF // 256
UP_ROUNDS = UP_CB // 3
DOWN_K = [8, 8, 6]
FFN_BLOCKS = 2 * UP_CB + 12
POS = positions()
SPLITS = []
for _s, (_n, _m, _a) in zip(STEPS, POS):
    if _s[0] in ('pt', 'wo') and _s[3] == 0:
        SPLITS.append((_n, BLK))
    elif _s[0] == 'ffn':
        SPLITS += [(_n + _b, BLK) for _b in range(2 * UP_CB)]
        SPLITS += [(_n + 2 * UP_CB + _b, DOWN_K[_b % 3] * 256) for _b in range(12)]
F0 = next(p[1] for t, p in zip(STEPS, POS) if t[0] == 'ffn')
BY_DVE = [F0 <= x < F0 + FFN_BLOCKS for x in range(len(SPLITS))]


def lo_of(m):
    return ("lo_made_dve" if BY_DVE[m] else "lo_made"), BY_DVE[:m + 1].count(BY_DVE[m])


M_END = sum(s[0] in ('pt', 'wo') and s[3] == 0 for s in STEPS) + FFN_BLOCKS


def rep(ap, at, n):
    a = ap.unsqueeze(at)
    shape = list(a.shape)
    shape[at] = n
    return a.broadcast_to(shape)


def program(nc, ins, outs, steps=None):
    steps = STEPS if steps is None else steps
    with ExitStack() as ctx:
        def sb(name, shape, dt=F32):
            return ctx.enter_context(nc.sbuf_tensor(name, shape, dt))

        sems = {}

        def S(name):
            if name not in sems:
                sems[name] = ctx.enter_context(nc.semaphore(name))
            return sems[name]

        bank = [ctx.enter_context(nc.psum_tensor(f"bank{i}", [P, 512], F32)) for i in range(8)]
        full = [S(f"bank_full{i}") for i in range(8)]
        read = [S(f"bank_read{i}") for i in range(8)]

        raw = sb("raw", [P, RAW, BLK])
        hi = [sb(f"hi{i}", [P, BLK], F32R) for i in range(SPLIT)]
        lo = [sb(f"lo{i}", [P, BLK], F32R) for i in range(SPLIT)]
        xT = sb("xT", [P, KT, N])
        UH = sb("UH", [P, KT, N], F32R)
        UL = sb("UL", [P, KT, N], F32R)
        mod = sb("mod", [P, 2, 6 * KT, 1 + NSEQ])
        pT = sb("pT", [P, 3, P])
        ident = sb("ident", [P, P])
        ones = sb("ones", [P, P])
        tri = sb("tri", [P, P])
        tri4 = sb("tri4", [P, P])
        blk4 = sb("blk4", [P, P])
        lows = sb("lows", [P, P])
        lows4 = sb("lows4", [P, P])
        lev = {s: sb(f"lev{s}", [P, P]) for s in [1] + LEVELS}
        lev1T = sb("lev1T", [P, P])
        sel = sb("sel", [P, 1 + NSEQ])
        mask8 = sb("mask8", [P, NSEQ])
        hm = sb("hm", [P, H])
        cT = sb("cT", [P, KT, 32])
        par = sb("par", [P, 2, 2, NU])
        wba = sb("wba", [P, 2, KT, 8])
        eps = sb("eps", [P, 3])
        small = sb("small", [P, 256])
        adas = sb("adas", [P, 512])
        pb = sb("pb", [8, N + P])
        KV8 = sb("KV8", [P, 2, P])
        CSC = sb("CSC", [P, CT, 2 * (1 + NSEQ)])

        splits = sum(1 for x in steps if x[0] in ('pt', 'wo') and x[3] == 0) + sum(
            FFN_BLOCKS for x in steps if x[0] == 'ffn')
        base = nc.sbuf_base
        base = (base + 63) // 64 * 64
        limit = nc.sbuf_usable_end

        def at(name, off, shape, dt=F32):
            n = 1
            for x in shape[1:]:
                n *= x
            assert base + 4 * (off + n) <= limit, (name, base + 4 * (off + n) - limit)
            return nc.alloc_sbuf_tensor_at(name, shape, dt, offset=base + 4 * off)

        U = P * NU
        o = 0
        EXT_O = o; o += 4096
        QKV_O = o; o += QT * N
        CH_O = o; o += CT * CE
        Z_O = o; o += H * N
        T_O = o; o += U
        TT_O = o; o += U
        ATT_O = o; o += U
        KD_O = o; o += U
        VB_O = o; o += U
        R_O = o; o += 5 * P
        WT_O = o; o += 4 * P
        WQ_O = o; o += 2 * P
        QD_O = o; o += 4 * P
        SP_O = o; o += 4 * P
        CB_O = o; o += (4 * DE + 7) // 8 * 8
        EG_O = o; o += 5 * P
        CT_O = o; o += 2 * N
        EXT = at("EXT", EXT_O, [P, QT, DE])
        SD = at("SD", EXT_O, [P, NSEQ, H, P])
        QKV = at("QKV", QKV_O, [P, QT, N])
        M = at("M", QKV_O, [P, NU, P])
        MT = at("MT", QKV_O + U, [P, NU, P])
        V = at("V", QKV_O + 2 * U, [P, NU, P])
        OT = at("OT", QKV_O, [P, H, N])
        RBO = at("RBO", QKV_O + U, [P, H, N])
        CH = at("CH", CH_O, [P, CT, CE])
        Z = at("Z", Z_O, [P, H, N])
        Tm = at("Tm", T_O, [P, NU, P])
        GS = at("GS", T_O, [P, NU, P])
        TTm = at("TTm", TT_O, [P, NU, P])
        GI = at("GI", TT_O, [P, NU, P])
        U32 = at("U32", T_O, [P, KT, N])
        NST = at("NST", EXT_O, [3 * 9, QT * P])
        NSC = at("NSC", T_O, [2 * 9, CT * P])
        ATT = at("ATT", ATT_O, [P, NU, P])
        RB = at("RB", ATT_O, [P, H, N])
        SIN = at("SIN", ATT_O, [3 * NSEQ, QT * P + CW])
        KD = at("KD", KD_O, [P, NU, P])
        SQ = at("SQ", KD_O, [P, H, N])
        VB = at("VB", VB_O, [P, NU, P])
        GU = at("GU", VB_O, [P, NU, P])
        VX = at("VX", VB_O, [P, NSEQ, P])
        R = at("R", R_O, [P, 5, P])
        WT = at("WT", WT_O, [P, H, P])
        WQ = at("WQ", WQ_O, [P, 2, P])
        QD = at("QD", QD_O, [P, H, P])
        SP = at("SP", SP_O, [P, H, P])
        CB = at("CB", CB_O, [P, 4, DE])
        X = at("X", CB_O, [P, NU, P])
        SQO = at("SQO", CB_O, [P, H, N])
        EG = at("EG", EG_O, [P, 5, P])
        CTM = at("CTM", CT_O, [P, 2, N])
        YTM = at("YTM", CT_O, [P, CE])
        CST = at("CST", WT_O, [P, QT, 27])
        XIN = at("XIN", 0, [P, 3, D])
        PIN = at("PIN", 3 * D, [P, 3, P])
        CIN = at("CIN", 3 * D + 3 * P, [1 + NSEQ, D])
        CSI = at("CSI", 3 * D + 3 * P + D, [1 + NSEQ, D])
        ROW = at("ROW", 3 * D + 3 * P + 2 * D, [1, 16])
        PBR = at("PBR", 3 * D + 3 * P + 2 * D + 16, [P, 2, 2, H])
        PTM = at("PTM", 3 * D + 3 * P + 2 * D + 32, [P, 4, H])
        XSQ = at("XSQ", TT_O, [P, KT, N])
        LNM = at("LNM", TT_O + KT * N, [P, N])
        LNR = at("LNR", TT_O + KT * N + N, [P, N])
        WTM = at("WTM", TT_O + KT * N + 2 * N, [P, 2, NS])
        UAB = at("UAB", TT_O + KT * N + 2 * N + 2 * NS, [P, 2, KT, 1 + NSEQ])
        XAB = at("XAB", TT_O + KT * N + 2 * N + 2 * NS + 2 * KT * (1 + NSEQ), [P, 2, KT])
        HH = at("HH", 0, [P, FT, N], F32R)
        HL = at("HL", FT * N, [P, FT, N], F32R)
        SG = at("SG", 2 * FT * N, [P, 2, N])
        HF = at("HF", 2 * FT * N + 2 * N, [P, 2, N])
        WTM2 = at("WTM2", 2 * FT * N + 4 * N, [P, 2, NS])
        XHH = at("XHH", 0, [P, XT, N], F32R)
        XHL = at("XHL", XT * N, [P, XT, N], F32R)
        o = 2 * XT * N
        hi_x = list(hi) + [at("hi2", o, [P, BLK], F32R)]; o += BLK
        XSG = at("XSG", o, [P, 2, N]); o += 2 * N
        XHF = at("XHF", o, [P, 2, N]); o += 2 * N
        GB = at("GB", o, [P, N]); o += N
        YTM2 = at("YTM2", o, [P, 2, NS]); o += 2 * NS
        assert o <= T_O
        DG = at("DG", o, [TT, NE, NTT, TT]); o += NE * N
        hi_x.append(at("hi3", o, [P, BLK], F32R)); o += BLK
        lo_x = list(lo)
        for i in (2, 3):
            lo_x.append(at(f"lo{i}", o, [P, BLK], F32R)); o += BLK
        YACC = at("YACC", o, [P, KT, N]); o += KT * N
        o = 0
        LG = at("LG", o, [NE, N]); o += N
        WR = at("WR", o, [P, KT, NE]); o += KT * NE
        BR = at("BR", o, [1, NE]); o += NE
        IDX = at("IDX", o, [P, NE]); o += NE
        PR = at("PR", o, [TT, NTT, NE]); o += NTT * NE
        EQ = at("EQ", o, [TT, NTT, NE]); o += NTT * NE
        SEL = at("SEL", o, [TT, NTT, NE]); o += NTT * NE
        SE2 = at("SE2", o, [TT, NTT, NE]); o += NTT * NE
        RED = at("RED", o, [TT, NTT])
        YO = at("YO", 0, [P, 3, D])

        block = ctx.enter_context(nc.Block())

        n_x = next(p[0] for t, p in zip(STEPS, POS) if t[0] == 'moe')
        slot_uses = [len(range(x, n_x, RAW)) for x in range(XRAW)]

        def x_cols(b):
            if b < XUP:
                return KT, min(256, DX - b // 2 * 256)
            return XD_K[b % 2], 256

        def x_raw(b, e):
            slot = b % XRAW
            kk, w_ = x_cols(b % XB)
            return raw[:, slot, 0:kk * w_], S(f"raw_full{slot}"), e * (16 * XB // XRAW) + 16 * (
                slot_uses[slot] + b // XRAW + 1)

        def lo_wait(eng, b, e):
            if b % 2 == 0:
                eng.wait_ge(S("lo_made"), e * (XB // 2) + (BY_DVE.count(False) + b // 2 + 1))
            else:
                eng.wait_ge(S("lo_made_dve"), e * (XB // 2) + (BY_DVE.count(True) + b // 2 + 1))

        def x_lo(eng, b, e, name):
            kk, w_ = x_cols(b % XB)
            src, _, _ = x_raw(b, e)
            eng.wait_ge(S("hi_made"), e * XB + (M_END + b + 1))
            q = b % XSPLIT
            eng.tensor_tensor(lo_x[q][:, 0:kk * w_], src, hi_x[q][:, 0:kk * w_].bitcast(F32),
                              ALU.subtract).then_inc(S(name), 1)

        def walk(fn):
            fills = [0] * 8
            for i, s in enumerate(steps):
                fn(s, i, list(fills))
                for b, n in banks_of(s).items():
                    fills[b] += n

        def w_src(s):
            l, m = s[1], s[2]
            if s[0] == 'pt':
                c = W_IN[m][1] * 256
                return ins['w_in'][l, :, c:c + 256].rearrange("(k p) n -> p k n", p=P)
            return ins['w_out'][l, :, m * 256:m * 256 + 256].rearrange("(k p) n -> p k n", p=P)

        @block.sync
        def _(sp):
            owner = []

            def load(dst_cols, src, kind):
                n = len(owner)
                if n >= RAW:
                    k, v = owner[n - RAW]
                    name, v = lo_of(v) if k == 'lo' else ("ada_used", v + 1)
                    sp.wait_ge(S(name), v)
                sp.dma_start(dst_cols, src).then_inc(S(f"raw_full{n % RAW}"), 16)
                owner.append(kind)

            def step(s, i, base):
                n, m, a = POS[i]
                k = s[0]
                if k == 'start':
                    for c in range(3):
                        rows = min(P, N - c * P)
                        src = ins['x_prompt'][0, c * P:(c + 1) * P, :] if c < 2 else \
                            ins['x_sample'].rearrange("s t d -> (s t) d")
                        sp.dma_start(XIN[0:rows, c, :], src).then_inc(S("x_loaded"), 16)
                    sp.dma_start(CIN[0:1, :], ins['c_prompt']).then_inc(S("c_loaded"), 16)
                    sp.dma_start(CIN[1:9, :], ins['c_sample']).then_inc(S("c_loaded"), 16)
                    sp.wait_ge(S("pin_cleared"), 1)
                    for dst, src in (
                            (PIN[0:96, 0, :], ins['b_ada'].rearrange("l (j p) -> (l j) p", p=P)),
                            (PIN[0:32, 1, :], ins['ln_g'].rearrange("l i (j p) -> (l i j) p", p=P)),
                            (PIN[32:64, 1, :], ins['ln_b'].rearrange("l i (j p) -> (l i j) p", p=P)),
                            (PIN[64:66, 1, :], ins['dn_norm_w']),
                            (PIN[96:120, 1, :], ins['conv_w'].rearrange("l k (j p) -> (l k j) p", p=P)),
                            (PIN[0:96, 2, :], ins['dn_conv_w'].rearrange("l k (j p) -> (l k j) p", p=P))):
                        sp.dma_start(dst, src).then_inc(S("p_loaded"), 16)
                    sp.dma_start(ROW[0:1, 0:8], ins['dt_bias'].rearrange("(o l) h -> o (l h)", o=1)).then_inc(S("p_loaded"), 16)
                    sp.dma_start(ROW[0:1, 8:16], ins['a_log'].rearrange("(o l) h -> o (l h)", o=1)).then_inc(S("p_loaded"), 16)
                    with nc.allow_non_contiguous_dma("eight columns of w_in"):
                        for l in range(DEPTH):
                            sp.dma_start(wba[:, l, :, :], ins['w_in'][l, :, PTOT - 8:PTOT].rearrange(
                                "(k p) n -> p k n", p=P)).then_inc(S("p_loaded"), 16)
                elif k == 'ada':
                    l, c = s[1], s[2]
                    for half in range(2):
                        src = ins['w_ada'][l, half * 512:half * 512 + 512, c * 512:c * 512 + 512]
                        slot = (n + half) % RAW
                        load(raw[:, slot, :].rearrange("p (k n) -> p k n", k=4),
                             src.rearrange("(k p) n -> p k n", p=P), ('ada', a + half))
                elif k in ('pt', 'wo') and s[3] == 0:
                    load(raw[:, n % RAW, :].rearrange("p (k n) -> p k n", k=KT), w_src(s), ('lo', m))
                elif k == 'ffn':
                    wg, wu, wd = ins['w_ff_gate'][0], ins['w_ff_up'][0], ins['w_ff_down'][0]

                    def up_src(w, j):
                        return w[:, bass.ds(j * 256, 256)].rearrange("(k p) n -> p k n", p=P)

                    def dst(n, kk):
                        return raw[:, n % RAW, 0:kk * 256].rearrange("p (k n) -> p k n", k=kk)
                    for b in range(6):
                        load(dst(n + b, KT), up_src((wg, wu)[b % 2], b // 2), ('lo', m + b))
                    with sp.Fori(1, UP_ROUNDS) as r:
                        for b in range(6):
                            name, v = lo_of(m + b)
                            sp.wait_ge(S(name), r * 6 + (v - 6))
                            sp.dma_start(dst(n + b, KT), up_src((wg, wu)[b % 2], r * 3 + b // 2)).then_inc(
                                S(f"raw_full{(n + b) % RAW}"), 16)
                    for b in range(6, 6 * UP_ROUNDS):
                        owner.append(('lo', m + b))
                    for b in range(6 * UP_ROUNDS, 2 * UP_CB):
                        load(dst(n + b, KT), up_src((wg, wu)[b % 2], b // 2), ('lo', m + b))
                    n, m = n + 2 * UP_CB, m + 2 * UP_CB
                    with sp.Fori(0, 2) as r:
                        for b in range(6):
                            kk = DOWN_K[b % 3]
                            k0 = 8 * (b % 3)
                            name, v = lo_of(m + b)
                            sp.wait_ge(S(name), r * 6 + (v - 6))
                            src = wd[k0 * P:(k0 + kk) * P, bass.ds((r * 2 + b // 3) * 256, 256)]
                            sp.dma_start(dst(n + b, kk), src.rearrange("(k p) n -> p k n", p=P)).then_inc(
                                S(f"raw_full{(n + b) % RAW}"), 16)
                    for b in range(12):
                        owner.append(('lo', m + b))
                elif k == 'moe':
                    wg, wu, wd = ins['w_exp_gate'], ins['w_exp_up'], ins['w_exp_down']

                    def x_load(b, e):
                        kk, w_ = x_cols(b)
                        dst, full_, _ = x_raw(b, 0)
                        if b < XUP:
                            src = (wg, wu)[b % 2][0, bass.ds(e, 1), :, b // 2 * 256:b // 2 * 256 + w_]
                        else:
                            k0, c0 = XD_K[0] * P * (b % 2), (b - XUP) // 2 * 256
                            src = wd[0, bass.ds(e, 1), k0:k0 + kk * P, c0:c0 + w_]
                        sp.dma_start(dst.rearrange("p (k n) -> p k n", k=kk),
                                     src.rearrange("o (k p) n -> p (o k) n", p=P)).then_inc(full_, 16)
                    for b in range(XB):
                        if b < XRAW:
                            kind, v = owner[max(x for x in range(len(owner)) if x % RAW == b)]
                            name, v = lo_of(v) if kind == 'lo' else ("ada_used", v + 1)
                            sp.wait_ge(S(name), v)
                        else:
                            lo_wait(sp, b - XRAW, 0)
                        x_load(b, 0)
                    with sp.Fori(1, NE) as e:
                        for b in range(XB):
                            lo_wait(sp, b - XRAW, e)
                            x_load(b, e)

            walk(step)

        @block.gpsimd
        def _(pool):
            count = [0]

            def then(ins_):
                count[0] += 1
                ins_.then_inc(S("pool_step"), 1)
                pool.wait_ge(S("pool_step"), count[0])

            def keep(t, pattern, base_, cm, op=ALU.is_ge, fill=0.0):
                then(pool.affine_select(out=t, in_=t, compare_op=op, fill=fill, base=base_,
                                        pattern=pattern, channel_multiplier=cm))

            pool.memset(PIN[:, :, :], 0.0).then_inc(S("pin_cleared"), 1)
            then(pool.memset(ones[:, :], 1.0))
            then(pool.memset(cT[:, :, :], 0.0))
            then(pool.memset(ident[:, :], 0.0))
            keep(ident[:, :], [[-1, P]], 0, 1, ALU.not_equal, 1.0)
            then(pool.memset(hm[:, :], 0.0))
            for h in range(H):
                then(pool.memset(hm[32 * h:32 * h + 32, h:h + 1], 1.0))
            then(pool.memset(sel[:, :], 0.0))
            for g in range(3):
                keep(sel[:, :], [[-1, 1 + NSEQ]], -32 * g, 1, ALU.not_equal, 1.0)
            pool.affine_select(out=sel[:, :], in_=sel[:, :], compare_op=ALU.not_equal, fill=1.0, base=-32 * 3,
                               pattern=[[-1, 1 + NSEQ]], channel_multiplier=1).then_inc(S("ident_made"), 1)
            pool.wait_ge(S("ident_made"), 1)
            for t in (tri, tri4, blk4, lows, lows4):
                then(pool.memset(t[:, :], 1.0))
            for t in (tri, tri4):
                keep(t[:, :], [[1, P]], 0, -1)
            for t in (lows, lows4):
                keep(t[:, :], [[-1, P]], -1, 1)
            for t in (tri4, blk4, lows4):
                keep(t[:, :], [[-4, 32], [0, 4]], 0, 1)
                keep(t[:, :], [[4, 32], [0, 4]], 3, -1)
            for s in [1] + LEVELS:
                v = lev[s][:, :].rearrange("p (b h j) -> p b h j", h=2, j=s)
                then(pool.memset(v[:, :, 0, :], 1.0))
                then(pool.memset(v[:, :, 1, :], 0.0))
                nb = P // 2 // s
                keep(v, [[-2 * s, nb], [0, 2], [0, s]], -s, 1)
                keep(v, [[2 * s, nb], [0, 2], [0, s]], 2 * s - 1, -1)
            v = lev1T[:, :].rearrange("p (b h) -> p b h", h=2)
            then(pool.memset(v[:, :, 0], 0.0))
            then(pool.memset(v[:, :, 1], 1.0))
            keep(v, [[-2, 64], [0, 2]], 0, 1)
            keep(v, [[2, 64], [0, 2]], 0, -1)
            then(pool.memset(mask8[:, :], 1.0))
            for h in range(H):
                v = mask8[32 * h:32 * h + 32, :]
                keep(v, [[-4, NSEQ]], 0, 1)
                keep(v, [[4, NSEQ]], 3, -1)
            then(pool.memset(eps[:, 0:1], LN_EPS))
            then(pool.memset(eps[:, 1:2], RMS_EPS))
            pool.memset(eps[:, 2:3], 1.0).then_inc(S("consts_made"), 1)

            def lo_part(n, m, cols=BLK):
                pool.wait_ge(S("hi_made"), m + 1)
                s_ = m % SPLIT
                pool.tensor_tensor(lo[s_][:, 0:cols], raw[:, n % RAW, 0:cols],
                                   hi[s_][:, 0:cols].bitcast(F32), ALU.subtract).then_inc(S("lo_made"), 1)

            def step(s, i, base):
                n, m, a = POS[i]
                k = s[0]
                if k in ('pt', 'wo') and s[3] == 0:
                    lo_part(n, m)
                elif k == 'moe':
                    def expert(e, last):
                        for b in range(XB):
                            if (b + 3) % 2 == 0 and not (last and b + 3 >= XB):
                                x_lo(pool, b + 3, e, "lo_made")
                    x_lo(pool, 0, 0, "lo_made")
                    x_lo(pool, 2, 0, "lo_made")
                    with pool.Fori(0, NE - 1) as e:
                        expert(e, False)
                    expert(NE - 1, True)

            walk(step)

        @block.tensor
        def _(pe):
            def fill(base, b, nth=1):
                if base[b] + nth - 1 > 0:
                    pe.wait_ge(read[b], base[b] + nth - 1)

            def mm3(out, wh, wl, xh, xl, start, stop):
                pe.matmul(out, wh, xh, start=start, stop=False)
                pe.matmul(out, wl, xh, start=False, stop=False)
                return pe.matmul(out, wh, xl, start=False, stop=stop)

            def tiles(base, b, t, m, kt, xh, xl, start=True, stop=True, nth=1, last=True):
                s_ = m % SPLIT
                wh = hi[s_][:, 0:kt * 256].rearrange("p (k n) -> p k n", k=kt)
                wl = lo[s_][:, 0:kt * 256].rearrange("p (k n) -> p k n", k=kt)
                for k in range(kt):
                    mm = mm3(bank[b][:, 0:N], wh[:, k, t * P:t * P + P], wl[:, k, t * P:t * P + P],
                             xh[:, k, :], xl[:, k, :], start and k == 0, stop and k == kt - 1)
                return mm

            def x_tiles(b, t, blk, xh, xl, start=True, stop=True):
                kk, w_ = x_cols(blk)
                q = blk % XSPLIT
                wh = hi_x[q][:, 0:kk * w_].rearrange("p (k n) -> p k n", k=kk)
                wl = lo_x[q][:, 0:kk * w_].rearrange("p (k n) -> p k n", k=kk)
                for k in range(kk):
                    mm = mm3(bank[b][:, 0:N], wh[:, k, t * P:t * P + P], wl[:, k, t * P:t * P + P],
                             xh[:, k, :], xl[:, k, :], start and k == 0, stop and k == kk - 1)
                return mm

            def sum_rows(src, b):
                return pe.matmul(bank[b][:, 0:N], ones[:, :], src, start=True, stop=True)

            def step(s, i, base):
                n, m, a = POS[i]
                k = s[0]
                l = s[1] if len(s) > 1 else 0
                if k == 'start':
                    pe.wait_ge(S("ident_made"), 1)
                    pe.wait_ge(S("x_loaded"), 48)
                    for d in range(KT):
                        for c in range(3):
                            rows = min(P, N - c * P)
                            mm = pe.transpose(bank[d][:, c * P:c * P + rows], XIN[0:rows, c, d * P:d * P + P],
                                              ident[0:rows, 0:rows])
                        mm.then_inc(full[d], 1)
                elif k == 'params':
                    pe.wait_ge(S("p_loaded"), 160)
                    fill(base, 0)
                    for c in range(3):
                        mm = pe.transpose(bank[0][:, c * P:c * P + P], PIN[:, c, :], ident[:, :])
                    mm.then_inc(full[0], 1)
                    fill(base, 1)
                    pe.matmul(bank[1][:, 0:16], ones[0:1, :], ROW[0:1, :], start=True, stop=True).then_inc(full[1], 1)
                    fill(base, 2)
                    pe.wait_ge(S("c_silu"), 1)
                    for d in range(KT):
                        mm = pe.transpose(bank[2][:, d * 9:d * 9 + 9], CSI[:, d * P:d * P + P], ident[0:9, 0:9])
                    mm.then_inc(full[2], 1)
                elif k == 'ada':
                    if a == 0:
                        pe.wait_ge(read[2], base[2])
                    fill(base, 4)
                    for half in range(2):
                        slot = (n + half) % RAW
                        pe.wait_ge(S(f"raw_full{slot}"), 16 * ((n + half) // RAW + 1))
                        for g in range(4):
                            mm = pe.matmul(bank[4][32 * g:32 * g + 32, :], cT[:, 4 * half + g, :],
                                           raw[:, slot, g * 512:g * 512 + 512], start=(half == 0), stop=(half == 1))
                        mm.then_inc(S("ada_used"), 1)
                elif k == 'adaT':
                    pe.wait_ge(read[4], base[4])
                    fill(base, 5)
                    for j in range(4):
                        mm = pe.matmul(bank[5][:, 9 * j:9 * j + 9], adas[:, j * P:j * P + P], sel[:, :], start=True, stop=True)
                    mm.then_inc(full[5], 1)
                elif k == 'ba':
                    pe.wait_ge(S("consts_made"), 1)
                    pe.wait_ge(S("u_made"), QTR * (2 * l + 1))
                    fill(base, 7)
                    for d in range(KT):
                        mm = pe.matmul(bank[7][0:8, 0:N], wba[:, l, d, :], U32[:, d, :], start=(d == 0), stop=(d == KT - 1))
                    mm.then_inc(full[7], 1)
                elif k == 'st_in':
                    pe.wait_ge(S("past_loaded"), 32 * (l + 1))
                    fill(base, 6)
                    for j in range(QT):
                        pe.transpose(bank[6][:, 24 * j:24 * j + 24], SIN[0:24, j * P:j * P + P], ident[0:24, 0:24])
                    for j in range(CT):
                        o_ = 24 * QT + 16 * j
                        mm = pe.transpose(bank[6][:, o_:o_ + 16], SIN[0:16, (QT + j) * P:(QT + j) * P + P], ident[0:16, 0:16])
                    mm.then_inc(full[6], 1)
                elif k == 'ba2':
                    fill(base, 7)
                    for c in range(3):
                        mm = pe.matmul(bank[7][:, 8 * c:8 * c + 8], pb[:, c * P:c * P + P], ident[0:8, 0:8], start=True, stop=True)
                    mm.then_inc(full[7], 1)
                elif k == 'pt':
                    if s[3] == 0:
                        pe.wait_ge(S("lo_made"), lo_of(m)[1])
                        if s[2] == 0:
                            pe.wait_ge(S("u_split"), 2 * l + 1)
                        mm_ = m
                    else:
                        mm_ = m - 1
                    fill(base, s[3])
                    mm = tiles(base, s[3], s[3], mm_, KT, UH, UL)
                    mm.then_inc(full[s[3]], 1)
                elif k == 'wo':
                    if s[3] == 0:
                        pe.wait_ge(S("lo_made"), lo_of(m)[1])
                        if s[2] == 0:
                            pe.wait_ge(S("mixed"), l + 1)
                        mm_ = m
                    else:
                        mm_ = m - 1
                    fill(base, s[3])
                    mm = tiles(base, s[3], s[3], mm_, KT, UH, UL)
                    mm.then_inc(full[s[3]], 1)
                elif k == 'ss':
                    pe.wait_ge(S("squared"), 2 * l + 1 + (s[2] == 'q'))
                    for h, b in enumerate((2, 3, 6, 7)):
                        fill(base, b)
                        sum_rows(SQ[:, h, :], b).then_inc(full[b], 1)
                elif k == 'gc':
                    pe.wait_ge(S("g_made"), l + 1)
                    fill(base, 2)
                    g = small[:, 64:64 + NU]
                    pe.matmul(bank[2][:, 0:8], tri[:, :], g[:, 0:8], start=True, stop=True)
                    pe.matmul(bank[2][:, 8:9], tri4[:, :], g[:, 8:9], start=True, stop=True)
                    pe.matmul(bank[2][:, 16:24], ones[:, :], g[:, 0:8], start=True, stop=True)
                    pe.matmul(bank[2][:, 24:25], blk4[:, :], g[:, 8:9], start=True, stop=True).then_inc(full[2], 1)
                    for b, u0, n_ in ((3, 0, 4), (6, 4, 4), (7, 8, 1)):
                        fill(base, b)
                        pe.matmul(bank[b][:, 0:n_ * P], ones[:, :], GU[:, u0:u0 + n_, :], start=True, stop=True).then_inc(full[b], 1)
                elif k == 'st_out':
                    pe.wait_ge(S("past_taken"), l + 1)
                    for q, b in enumerate((2, 3, 6)):
                        fill(base, b)
                        for j in range(4):
                            mm = pe.transpose(bank[b][0:27, j * P:j * P + P], CST[:, 4 * q + j, :], ident[:, :])
                        mm.then_inc(full[b], 1)
                elif k == 'tok':
                    for t0, b3 in ((H, (2, 3, 6)), (2 * H, (7, 2, 3))):
                        if t0 == H:
                            pe.wait_ge(S("k_normed"), l + 1)
                        else:
                            pe.wait_ge(S("v8_made"), l + 1)
                        for q, b in enumerate(b3):
                            nth = 2 if (t0 == 2 * H and b in (2, 3)) else 1
                            fill(base, b, nth)
                            us = [4 * q + x for x in range(4)] if q < 2 else [8]
                            for x, u in enumerate(us):
                                src = KV8[:, 0 if t0 == H else 1, :] if u == DEC else \
                                    QKV[:, t0 + u // 2, (u % 2) * P:(u % 2) * P + P]
                                mm = pe.transpose(bank[b][:, x * P:x * P + P], src, ident[:, :])
                            mm.then_inc(full[b], 1)
                elif k == 'att' or k == 'kk':
                    if k == 'att':
                        pe.wait_ge(S("q_normed"), l + 1)
                    for q, b in enumerate((6, 7, 2) if k == 'att' else (3, 6, 7)):
                        fill(base, b)
                        for x, u in enumerate([4 * q + y for y in range(4)] if q < 2 else [8]):
                            t0 = 0 if k == 'att' else H
                            if u == DEC:
                                wk, xq = KV8[:, 0, :], QKV[:, t0:t0 + H, NP_:N]
                            else:
                                cols = slice((u % 2) * P, (u % 2) * P + P)
                                wk, xq = QKV[:, H + u // 2, cols], QKV[:, t0 + u // 2, cols]
                            mm = pe.matmul(bank[b][:, x * P:x * P + P], wk, xq, start=True, stop=True)
                        mm.then_inc(full[b], 1)
                elif k == 'mt':
                    pe.wait_ge(S("m_made"), l + 1)
                    for q, b in enumerate((2, 3, 6)):
                        fill(base, b)
                        for x, u in enumerate([4 * q + y for y in range(4)] if q < 2 else [8]):
                            mm = pe.transpose(bank[b][:, x * P:x * P + P], M[:, u, :], ident[:, :])
                        mm.then_inc(full[b], 1)
                elif k == 'X':
                    b, _, us = GRP[s[3]]
                    if s[2] == 2:
                        pe.wait_ge(S("t_made"), l + 1)
                    fill(base, b)
                    for x, u in enumerate(us):
                        mm = pe.matmul(bank[b][:, x * P:x * P + P], MT[:, u, :], Tm[:, u, :], start=True, stop=True)
                    mm.then_inc(full[b], 1)
                elif k == 'Y':
                    b, bt, us = GRP[s[3]]
                    pe.wait_ge(read[b], base[b])
                    if s[2] < 64:
                        fill(base, b)
                        for x, u in enumerate(us):
                            mm = pe.matmul(bank[b][:, x * P:x * P + P], TTm[:, u, :], X[:, u, :], start=True, stop=True)
                        mm.then_inc(full[b], 1)
                    fill(base, bt)
                    for x, u in enumerate(us):
                        mm = pe.matmul(bank[bt][:, x * P:x * P + P], X[:, u, :], TTm[:, u, :], start=True, stop=True)
                    mm.then_inc(full[bt], 1)
                elif k == 'wt':
                    for b in (3, 7):
                        pe.wait_ge(read[b], base[b])
                    fill(base, 2)
                    for h in range(H):
                        mm = pe.matmul(bank[2][:, h * P:h * P + P], R[:, h, :], TTm[:, 2 * h + 1, :], start=True, stop=True)
                    mm.then_inc(full[2], 1)
                    fill(base, 3)
                    pe.matmul(bank[3][:, 0:P], R[:, 4, :], TTm[:, DEC, :], start=True, stop=True).then_inc(full[3], 1)
                    fill(base, 6)
                    for h in range(H):
                        mm = pe.matmul(bank[6][:, h * P:h * P + P], TTm[:, 2 * h, :], VB[:, 2 * h, :], start=True, stop=True)
                    mm.then_inc(full[6], 1)
                elif k == 'c0':
                    pe.wait_ge(read[6], base[6])
                    pe.wait_ge(S("mem_loaded"), 16 * (l + 1))
                    fill(base, 7)
                    for h in range(H):
                        mm = pe.matmul(bank[7][:, h * P:h * P + P], V[:, 2 * h, :], ATT[:, 2 * h, :], start=True, stop=True)
                    mm.then_inc(full[7], 1)
                    fill(base, 2)
                    for h in range(H):
                        mm = pe.matmul(bank[2][:, h * P:h * P + P], KD[:, 2 * h, :], V[:, 2 * h, :], start=True, stop=True)
                    mm.then_inc(full[2], 1)
                    fill(base, 3)
                    out = bank[3][:, 0:2 * P].rearrange("p (x j) -> p x j", x=2)
                    for h in range(H):
                        for q in range(NSEQ):
                            j = h * NS + q * NT
                            mm = pe.matmul(out[:, :, j:j + NT], SD[:, q, h, :], WQ[:, :, j:j + NT], start=True, stop=True)
                    mm.then_inc(full[3], 1)
                elif k == 'c1':
                    pe.wait_ge(read[2], base[2])
                    fill(base, 6)
                    for h in range(H):
                        pe.matmul(bank[6][:, h * P:h * P + P], TTm[:, 2 * h + 1, :], VB[:, 2 * h + 1, :], start=True, stop=False)
                        mm = pe.matmul(bank[6][:, h * P:h * P + P], WT[:, h, :], SP[:, h, :], start=False, stop=True)
                    mm.then_inc(full[6], 1)
                    fill(base, 3)
                    pe.matmul(bank[3][:, 0:P], TTm[:, DEC, :], VB[:, DEC, :], start=True, stop=False)
                    pe.matmul(bank[3][:, 0:P], WQ[:, 0, :], ident[:, :], start=False, stop=True).then_inc(full[3], 1)
                elif k == 'c2':
                    pe.wait_ge(read[6], base[6])
                    pe.wait_ge(read[3], base[3])
                    fill(base, 7)
                    for h in range(H):
                        pe.matmul(bank[7][:, h * P:h * P + P], SP[:, h, :], QD[:, h, :], start=True, stop=False)
                        mm = pe.matmul(bank[7][:, h * P:h * P + P], V[:, 2 * h + 1, :], ATT[:, 2 * h + 1, :], start=False, stop=True)
                    mm.then_inc(full[7], 1)
                    fill(base, 2)
                    for h in range(H):
                        mm = pe.matmul(bank[2][:, h * P:h * P + P], KD[:, 2 * h + 1, :], V[:, 2 * h + 1, :], start=True, stop=True)
                    mm.then_inc(full[2], 1)
                    fill(base, 3)
                    pe.matmul(bank[3][:, 0:P], V[:, DEC, :], ATT[:, DEC, :], start=True, stop=True).then_inc(full[3], 1)
                elif k == 'su':
                    h = s[2]
                    pe.wait_ge(S("vx_made"), l + 1)
                    for q, b in enumerate((2, 3) if h % 2 == 0 else (6, 7)):
                        fill(base, b)
                        pe.matmul(bank[b][:, :], KD[32 * h:32 * h + 32, DEC, :],
                                  VX[32 * h:32 * h + 32, 4 * q:4 * q + 4, :], start=True, stop=True).then_inc(full[b], 1)
                elif k == 'on':
                    pe.wait_ge(S("o_squared"), l + 1)
                    for h, b in enumerate((2, 3, 6, 7)):
                        fill(base, b)
                        sum_rows(SQO[:, h, :], b).then_inc(full[b], 1)
                elif k == 'cs_out':
                    pe.wait_ge(S("cs_taken"), l + 1)
                    fill(base, 6)
                    for j in range(CT):
                        mm = pe.transpose(bank[6][0:18, j * P:j * P + P], CSC[:, j, :], ident[:, :])
                    mm.then_inc(full[6], 1)
                elif k == 'lnm':
                    which = 2 * l + s[2]
                    pe.wait_ge(S("x_added"), which + 1)
                    fill(base, 6)
                    for d in range(KT):
                        mm = pe.matmul(bank[6][:, 0:N], ones[:, :], xT[:, d, :], start=(d == 0), stop=(d == KT - 1))
                    mm.then_inc(full[6], 1)
                elif k == 'lnv':
                    which = 2 * l + s[2]
                    fill(base, 7)
                    for d in range(KT):
                        if d % 2 == 0:
                            pe.wait_ge(S("x_squared"), QTR * which + d // 2 + 1)
                        mm = pe.matmul(bank[7][:, 0:N], ones[:, :], XSQ[:, d, :], start=(d == 0), stop=(d == KT - 1))
                    mm.then_inc(full[7], 1)
                elif k == 'ffn':
                    for b in range(6):
                        fill(base, b)
                    pe.wait_ge(S("u_split"), 2 * l + 2)

                    def up_block(r, b, first):
                        name, v = lo_of(m + b)
                        pe.wait_ge(S(name), r * 6 + v)
                        pair = b % 2
                        c = b // 2
                        if not (first and c == 0):
                            pe.wait_ge(S("ffn_gate_read") if pair == 0 else S("ffn_up_read"), r * 3 + c)
                        for t in range(2):
                            mm = tiles(None, 2 * pair + t, t, m + b, KT, UH, UL)
                        mm.then_inc(S("ffn_mm"), 1)
                    for b in range(6):
                        up_block(0, b, True)
                    with pe.Fori(1, UP_ROUNDS) as r:
                        for b in range(6):
                            up_block(r, b, False)
                    for b in range(6 * UP_ROUNDS, 2 * UP_CB):
                        up_block(0, b, False)
                    m2 = m + 2 * UP_CB
                    pe.wait_ge(S("ffn_gate_read"), UP_CB)
                    with pe.Fori(0, 2) as r:
                        for c in range(2):
                            for q in range(3):
                                b = 3 * c + q
                                name, v = lo_of(m2 + b)
                                pe.wait_ge(S(name), r * 6 + v)
                                pe.wait_ge(S("h_split"), 4 * q + DOWN_K[q] // 2)
                                if q == 0:
                                    pe.wait_ge(S(f"down_read{c}"), r + 1)
                                for t in range(2):
                                    mm = tiles(None, 4 * c + t, t, m2 + b, DOWN_K[q], HH[:, 8 * q:8 * q + DOWN_K[q], :],
                                               HL[:, 8 * q:8 * q + DOWN_K[q], :], start=(q == 0), stop=(q == 2))
                                mm.then_inc(S("ffn_mm"), 1)
                elif k == 'moe':
                    for b in range(8):
                        fill(base, b)
                    pe.wait_ge(S("u_made"), QTR * (2 * l + 2))
                    pe.wait_ge(S("router_loaded"), 32)
                    for d in range(KT):
                        mm = pe.matmul(bank[6][0:NE, 0:N], WR[:, d, :], U32[:, d, :], start=(d == 0), stop=(d == KT - 1))
                    mm.then_inc(S("logits_made"), 1)
                    pe.wait_ge(S("logits_copied"), 1)
                    for c in range(NTT):
                        pe.matmul(bank[7][0:TT, NE * c:NE * c + NE], LG[:, c * TT:c * TT + TT], ident[0:NE, 0:NE],
                                  start=True, stop=False)
                        mm = pe.matmul(bank[7][0:TT, NE * c:NE * c + NE], ones[0:1, 0:TT], BR[0:1, :], start=False, stop=True)
                    mm.then_inc(S("logits_turned"), 1)
                    pe.wait_ge(S("u_split"), 2 * l + 2)
                    pe.wait_ge(S("router_read"), 1)
                    with pe.Fori(0, NE) as e:
                        for b in range(XB):
                            j = b // 2
                            kk, w_ = x_cols(b)
                            if b == XUP - 2:
                                pe.wait_ge(S("x_gate_read"), e * XCB + j)
                                pe.wait_ge(S("dg_made"), 1)
                                for c in range(NTT):
                                    mm = pe.matmul(bank[1][:, c * TT:c * TT + TT], ones[0:TT, :],
                                                   DG[:, bass.ds(e, 1), c, :], start=True, stop=True)
                                mm.then_inc(S("gb_summed"), 1)
                            lo_wait(pe, b, e)
                            if b < XUP:
                                if j > 0:
                                    pe.wait_ge(S("x_gate_read") if b % 2 == 0 else S("x_up_read"), e * XCB + j)
                                for t in range(w_ // P):
                                    mm = x_tiles(2 * (b % 2) + t, t, b, UH, UL)
                            else:
                                cb = (b - XUP) // 2
                                k0 = XD_K[0] * (b % 2)
                                if b < XUP + 2:
                                    pe.wait_ge(S("xh_split"), e * XCB + (XD_K[0] // 2 if b == XUP else XCB))
                                if b % 2 == 0 and cb > 1:
                                    pe.wait_ge(S("y_scaled"), e * XDB + (cb - 1))
                                for t in range(2):
                                    mm = x_tiles(4 + 2 * (cb % 2) + t, t, b, XHH[:, k0:k0 + kk, :], XHL[:, k0:k0 + kk, :],
                                                 b % 2 == 0, b % 2 == 1)
                            mm.then_inc(S("x_mm"), 1)
                elif k == 'out':
                    for c in range(3):
                        rows = min(P, N - c * P)
                        for half in range(2):
                            b = OUT_BANKS[2 * c + half]
                            pe.wait_ge(S("x_normed"), half + 1)
                            fill(base, b)
                            for j in range(4):
                                mm = pe.transpose(bank[b][0:rows, j * P:j * P + P], xT[:, 4 * half + j, c * P:c * P + rows], ident[:, :])
                            mm.then_inc(full[b], 1)

            walk(step)

        @block.scalar
        def _(act):
            def got(base, b, nth=1):
                act.wait_ge(full[b], base[b] + nth)

            stores = {}

            def store(dst, src, name):
                stores[name] = stores.get(name, 0) + 16
                act.dma_start(dst, src).then_inc(S(name), 16)

            def hi_part(m):
                n, cols = SPLITS[m]
                act.wait_ge(S(f"raw_full{n % RAW}"), 16 * (n // RAW + 1))
                act.activation(hi[m % SPLIT][:, 0:cols], raw[:, n % RAW, 0:cols], ACT.Copy).then_inc(S("hi_made"), 1)

            def rsqrt(dst, src_banks, base, scale, eps_col, name):
                for i_, b in enumerate(src_banks):
                    got(base, b)
                    act.activation(dst[:, i_, :] if dst.shape[1] != N else dst[:, :], bank[b][:, 0:N], ACT.Ln,
                                   bias=eps[:, eps_col:eps_col + 1], scale=scale).then_inc(read[b], 1)
                act.wait_ge(read[src_banks[-1]], base[src_banks[-1]] + 1)
                act.activation(dst[:, :, :] if dst.shape[1] != N else dst[:, :],
                               dst[:, :, :] if dst.shape[1] != N else dst[:, :], ACT.Exp, scale=-0.5).then_inc(S(name), 1)

            def step(s, i, base):
                n, m, a = POS[i]
                k = s[0]
                l = s[1] if len(s) > 1 else 0
                if k == 'start':
                    act.wait_ge(S("c_loaded"), 32)
                    act.activation(CSI[:, :], CIN[:, :], ACT.Silu).then_inc(S("c_silu"), 1)
                    for d in range(1, KT, 2):
                        got(base, d)
                        act.copy(xT[:, d, :], bank[d][:, 0:N]).then_inc(read[d], 1)
                elif k == 'params':
                    act.wait_ge(S("par_made"), 1)
                    act.activation(par[:, 1, :, :], par[:, 1, :, :], ACT.Exp).then_inc(S("a_exp"), 1)
                elif k == 'ada':
                    act.wait_ge(S("ada_used"), a + 2)
                    if (l, s[2]) != (0, 0):
                        act.wait_ge(full[5], base[5])
                    act.copy(adas[:, :], bank[4][:, :]).then_inc(read[4], 1)
                elif k == 'u':
                    if s == ('u', 0, 1) and m + 1 < splits:
                        hi_part(m)
                        hi_part(m + 1)
                    for q in range(QTR):
                        act.wait_ge(S("u_made"), QTR * (2 * l + s[2]) + q + 1)
                        act.activation(UH[:, 2 * q:2 * q + 2, :], U32[:, 2 * q:2 * q + 2, :], ACT.Copy).then_inc(S("uh_made"), 1)
                    if s == ('u', 0, 0):
                        act.activation(xT[:, :, :], xT[:, :, :], ACT.Copy, scale=ALPHA).then_inc(S("x_scaled"), 1)
                    else:
                        for d in range(KT):
                            mm = act.activation(xT[:, d, :], xT[:, d, :], ACT.Identity, bias=XAB[:, 1, d:d + 1],
                                                scale=XAB[:, 0, d:d + 1])
                        mm.then_inc(S("x_scaled"), 1)
                    if s[2] == 0:
                        if l == 0:
                            hi_part(0)
                            hi_part(1)
                        act.wait_ge(S("x_scaled"), 2 * l + 1)
                        act.dma_start(SIN[0:24, 0:QT * P], ins['state_dn_conv'][l].rearrange("s k c -> (s k) c")).then_inc(S("past_loaded"), 16)
                        act.dma_start(SIN[0:16, QT * P:], ins['state_conv'][l].rearrange("s k c -> (s k) c")).then_inc(S("past_loaded"), 16)
                elif k == 'ba':
                    got(base, 7)
                    act.copy(pb[:, 0:N - NS], bank[7][0:8, 0:NP_])
                    act.copy(pb[:, NP_:NP_ + P].rearrange("p (h t) -> p h t", h=H), rep(bank[7][0:8, NP_:N], 1, H)).then_inc(read[7], 1)
                elif k in ('pt', 'wo'):
                    t = s[3]
                    b = t
                    if k == 'pt':
                        what, blk_ = W_IN[s[2]]
                        if what in 'qkv':
                            j = (blk_ - 6) * 2 + t
                            if s[2] == 0 and t == 0:
                                act.wait_ge(S("ext_cleared"), l + 1)
                            got(base, b)
                            act.copy(EXT[:, j, DK - 1:DK - 1 + NP_], bank[b][:, 0:NP_])
                            mm = act.copy(EXT[:, j, DS0:].rearrange("p (s t) -> p s t", s=NSEQ)[:, :, DK - 1:],
                                          bank[b][:, NP_:N].rearrange("p (s t) -> p s t", s=NSEQ))
                            mm.then_inc(read[b], 1)
                        elif what == 'z':
                            got(base, b)
                            act.activation(Z[:, (blk_ - 12) * 2 + t, :], bank[b][:, 0:N], ACT.Silu).then_inc(read[b], 1)
                        elif what == 'c':
                            got(base, b)
                            act.wait_ge(read[t], base[t])
                            act.copy(CTM[:, t, :], bank[b][:, 0:N]).then_inc(read[b], 1)
                    if t == 1:
                        act.wait_ge(full[1], base[1] + 1)
                        if m + 1 < splits and not (k == 'wo' and s[2] > 1):
                            hi_part(m + 1)
                elif k == 'conv':
                    g = 'kqv'.index(s[2])
                    t0 = {'q': 0, 'k': H, 'v': 2 * H}[s[2]]
                    act.wait_ge(S("conv_made"), 3 * l + g + 1)
                    act.activation(QKV[:, t0:t0 + H, 0:NP_], CB[:, :, 0:NP_], ACT.Silu)
                    for h in range(H):
                        src = CB[:, h, DS0:].rearrange("p (s t) -> p s t", s=NSEQ)[:, :, 0:NT]
                        mm = act.activation(QKV[:, t0 + h, NP_:N].rearrange("p (s t) -> p s t", s=NSEQ), src, ACT.Silu)
                    mm.then_inc(S("conv_done"), 1)
                    if s[2] != 'v':
                        act.wait_ge(S("conv_done"), 3 * l + g + 1)
                        if s[2] == 'q':
                            act.wait_ge(S("k_normed"), l + 1)
                        act.activation(SQ[:, :, :], QKV[:, t0:t0 + H, :], ACT.Square).then_inc(S("squared"), 1)
                elif k == 'ss':
                    if s[2] == 'q':
                        act.wait_ge(S("k_normed"), l + 1)
                    rsqrt(RB, (2, 3, 6, 7), base, 1.0, 1, "norm_made")
                elif k == 'ba2':
                    w = lambda j, n_=NU: small[:, j:j + n_]
                    act.wait_ge(S("ab_made"), l + 1)
                    act.activation(w(96), w(0), ACT.Exp, scale=-1.0)
                    act.activation(w(112), w(32), ACT.Exp, scale=-1.0).then_inc(S("gate_exps"), 1)
                    act.wait_ge(S("gate_exps"), l + 1)
                    act.activation(w(128), w(112), ACT.Ln, bias=eps[:, 2:3]).then_inc(S("gate_ln"), 1)
                elif k == 'gc':
                    w = lambda j, n_=NU: small[:, j:j + n_]
                    for b, j, src in ((3, 0, bank[3][:, :].rearrange("p (h c t) -> p h c t", h=2, c=2)[:, :, 1, :]),
                                      (6, 2, bank[6][:, :].rearrange("p (h c t) -> p h c t", h=2, c=2)[:, :, 1, :]),
                                      (7, 4, bank[7][:, 0:P].unsqueeze(1))):
                        got(base, b)
                        mm = act.activation(EG[:, j:j + src.shape[1], :], src, ACT.Exp)
                    mm.then_inc(S("eg_made"), 1)
                    act.wait_ge(S("gc_made"), l + 1)
                    act.activation(w(176), w(144), ACT.Exp)
                    act.activation(w(192), w(160), ACT.Exp).then_inc(S("decays"), 1)
                    act.wait_ge(S("gs_diff"), l + 1)
                    act.activation(GS[:, :, :], GS[:, :, :], ACT.Exp, scale=-1.0)
                    act.activation(GI[:, :, :], GI[:, :, :], ACT.Exp).then_inc(S("gammas"), 1)
                elif k == 'st_out':
                    for q, b in enumerate((2, 3, 6)):
                        got(base, b)
                        mm = act.copy(NST[:, q * 512:q * 512 + 512], bank[b][0:27, :])
                        mm.then_inc(read[b], 1)
                    act.wait_ge(read[6], base[6] + 1)
                    store(outs[3][l, 0], NST[0:3, :], "nst_stored")
                    store(outs[6][l].rearrange("s k c -> (s k) c"), NST[3:27, :], "nst_stored")
                elif k == 'tok':
                    for t0, b3 in ((H, (2, 3, 6)), (2 * H, (7, 2, 3))):
                        dst, sc = (KD, 192) if t0 == H else (VB, 208)
                        for q, b in enumerate(b3):
                            nth = 2 if (t0 == 2 * H and b in (2, 3)) else 1
                            got(base, b, nth)
                            for x, u in enumerate([4 * q + y for y in range(4)] if q < 2 else [8]):
                                mm = act.activation(dst[:, u, :], bank[b][:, x * P:x * P + P], ACT.Copy,
                                                    scale=small[:, sc + u:sc + u + 1])
                            if t0 == H:
                                mm.then_inc(S("kd_bank"), 1)
                            else:
                                mm.then_inc(read[b], 1)
                elif k == 'mt':
                    for q, b in enumerate((2, 3, 6)):
                        got(base, b)
                        us = slice(4 * q, 4 * q + 4) if q < 2 else slice(8, 9)
                        w_ = (us.stop - us.start) * P
                        act.copy(MT[:, us, :], bank[b][:, 0:w_]).then_inc(read[b], 1)
                elif k == 'X':
                    if s[2] == 4 and s[3] == 'A':
                        act.wait_ge(S("nst_stored"), 32 * (l + 1))
                        act.dma_start(SD[:, :, :, :], ins['state_dn'][l].rearrange("s h k v -> k s h v")).then_inc(S("mem_loaded"), 16)
                elif k == 'wt':
                    got(base, 2)
                    act.activation(WT[:, :, :], bank[2][:, :], ACT.Copy, scale=-1.0).then_inc(read[2], 1)
                    got(base, 3)
                    act.copy(WQ[:, 0, :], bank[3][:, 0:P]).then_inc(read[3], 1)
                elif k == 'c0':
                    got(base, 7)
                    act.copy(OT[:, :, 0:P], bank[7][:, :].rearrange("p (h t) -> p h t", h=H)).then_inc(read[7], 1)
                elif k == 'c2':
                    got(base, 7)
                    act.copy(OT[:, :, P:NP_], bank[7][:, :].rearrange("p (h t) -> p h t", h=H)).then_inc(read[7], 1)
                    act.wait_ge(read[7], base[7] + 1)
                    act.wait_ge(S("o_dec"), l + 1)
                    act.activation(SQO[:, :, :], OT[:, :, :], ACT.Square).then_inc(S("o_squared"), 1)
                    act.wait_ge(S("s2_made"), l + 1)
                    store(outs[4][l, 0].rearrange("h k v -> k h v"), SP[:, :, :], "sp_stored")
                elif k == 'on':
                    rsqrt(RBO, (2, 3, 6, 7), base, 1.0 / P, 1, "o_norm")
                    act.wait_ge(S("sd_made"), l + 1)
                    store(outs[7][l].rearrange("s h k v -> k s h v"), SD[:, :, :, :], "sd_stored")
                elif k == 'cs_out':
                    got(base, 6)
                    act.copy(NSC[:, :], bank[6][0:18, :]).then_inc(read[6], 1)
                    act.wait_ge(read[6], base[6] + 1)
                    store(outs[2][l, 0], NSC[0:2, :], "nsc_stored")
                    store(outs[5][l].rearrange("s k c -> (s k) c"), NSC[2:18, :], "nsc_stored")
                elif k == 'mix':
                    act.wait_ge(S("y_made"), l + 1)
                    for j in range(CT):
                        act.activation(UH[:, j, :], CH[:, j, 0:N], ACT.Copy)
                    act.wait_ge(S("o_gated"), l + 1)
                    act.activation(UH[:, CT:KT, :], OT[:, :, :], ACT.Copy).then_inc(S("mixed_hi"), 1)
                elif k == 'lnm':
                    for q in range(QTR):
                        act.wait_ge(S("x_centred"), QTR * (2 * l + s[2]) + q + 1)
                        act.activation(XSQ[:, 2 * q:2 * q + 2, :], xT[:, 2 * q:2 * q + 2, :], ACT.Square).then_inc(S("x_squared"), 1)
                elif k == 'lnv':
                    rsqrt(LNR, (7,), base, 1.0 / D, 0, "ln_rstd")
                elif k == 'ffn':
                    def after(r, b):
                        act.wait_ge(S("ffn_mm"), r * 6 + (b + 1))
                        hb = m + b + 2
                        act.wait_ge(S(f"raw_full{(n + b + 2) % RAW}"), r * 16 + 16 * ((n + b + 2) // RAW + 1))
                        act.activation(hi[hb % SPLIT][:, :], raw[:, (n + b + 2) % RAW, :], ACT.Copy).then_inc(S("hi_made"), 1)
                        c = r * 3 + b // 2
                        if b % 2 == 0:
                            if b >= 2 or not isinstance(r, int) or r > 0:
                                act.wait_ge(S("ffn_up_read"), c)
                            for t in range(2):
                                mm = act.activation(SG[:, t, :], bank[t][:, 0:N], ACT.Silu)
                            mm.then_inc(S("ffn_gate_read"), 1)
                        else:
                            act.wait_ge(S("hf_made"), c + 1)
                            act.activation(HH[:, bass.ds(c * 2, 2), :], HF[:, :, :], ACT.Copy).then_inc(S("hh_made"), 1)
                    for b in range(6):
                        after(0, b)
                    with act.Fori(1, UP_ROUNDS) as r:
                        for b in range(6):
                            after(r, b)
                    for b in range(6 * UP_ROUNDS, 2 * UP_CB):
                        after(0, b)
                    for b in range(2 * UP_CB, FFN_BLOCKS):
                        act.wait_ge(S("ffn_mm"), b + 1)
                        if m + b + 2 < splits:
                            hi_part(m + b + 2)
                elif k == 'moe':
                    act.dma_start(WR[:, :, :], ins['w_router'][0].rearrange("(k p) n -> p k n", p=P)).then_inc(S("router_loaded"), 16)
                    act.dma_start(BR[:, :], ins['b_router']).then_inc(S("router_loaded"), 16)

                    def x_hi(b, e):
                        src, full_, v = x_raw(b, e)
                        q = b % XSPLIT
                        act.wait_ge(full_, v)
                        if b >= XSPLIT - 1:
                            act.wait_ge(S("x_mm"), e * XB + max(b - XSPLIT + 1, 1))
                        act.activation(hi_x[q][:, 0:src.shape[1]], src, ACT.Copy).then_inc(S("hi_made"), 1)

                    def expert(e, last):
                        for b in range(XB):
                            if not (last and b + 3 >= XB):
                                x_hi(b + 3, e)
                            j = b // 2
                            n_t = x_cols(b)[1] // P
                            if b == XUP - 2:
                                act.wait_ge(S("gb_summed"), e + 1)
                                act.copy(GB[:, :], bank[1][:, 0:N]).then_inc(S("gb_made"), 1)
                            if b < XUP and b % 2 == 0:
                                act.wait_ge(S("x_mm"), e * XB + (b + 1))
                                for t in range(n_t):
                                    mm = act.activation(XSG[:, t, :], bank[t][:, 0:N], ACT.Silu)
                                mm.then_inc(S("x_gate_read"), 1)
                            elif b < XUP:
                                act.wait_ge(S("xhf_made"), e * XCB + (j + 1))
                                act.activation(XHH[:, 2 * j:2 * j + n_t, :], XHF[:, 0:n_t, :], ACT.Copy).then_inc(S("xhh_made"), 1)
                    x_hi(0, 0)
                    x_hi(1, 0)
                    act.wait_ge(S("logits_made"), 1)
                    act.copy(LG[:, :], bank[6][0:NE, 0:N]).then_inc(S("logits_copied"), 1)
                    x_hi(2, 0)
                    act.wait_ge(S("logits_shifted"), 1)
                    act.activation(PR[:, :, :], PR[:, :, :], ACT.Exp).then_inc(S("router_exp"), 1)
                    with act.Fori(0, NE - 1) as e:
                        expert(e, False)
                    expert(NE - 1, True)
                elif k == 'out':
                    for c in range(3):
                        rows = min(P, N - c * P)
                        for half in range(2):
                            b = OUT_BANKS[2 * c + half]
                            got(base, b)
                            act.copy(YO[0:rows, c, half * 512:half * 512 + 512], bank[b][0:rows, :]).then_inc(read[b], 1)
                        act.wait_ge(read[b], base[b] + 1)
                        dst = outs[0][0, c * P:c * P + P, :] if c < 2 else outs[1].rearrange("s t d -> (s t) d")
                        store(dst, YO[0:rows, c, :], "y_stored")

            walk(step)
            for name, v in stores.items():
                act.wait_ge(S(name), v)

        @block.vector
        def _(dve):
            count = [0]

            def then(ins_):
                count[0] += 1
                ins_.then_inc(S("dve_step"), 1)
                dve.wait_ge(S("dve_step"), count[0])

            def got(base, b, nth=1):
                dve.wait_ge(full[b], base[b] + nth)

            def halves(row, width):
                s0 = NP_ + width
                return row[:, width:s0], row[:, s0:].rearrange("p (s t) -> p s t", s=NSEQ)[:, :, width:]

            def add_scaled(src, d, l, g, tmp):
                gate = mod[:, l, g * KT + d, :]
                dve.scalar_tensor_tensor(xT[:, d, 0:NP_], src[:, 0:NP_], gate[:, 0:1], xT[:, d, 0:NP_],
                                         ALU.mult, ALU.add)
                then(dve.tensor_tensor(tmp.rearrange("p (s t) -> p s t", s=NSEQ),
                                       src[:, NP_:N].rearrange("p (s t) -> p s t", s=NSEQ),
                                       rep(gate[:, 1:], 2, NT), ALU.mult))
                return dve.tensor_tensor(xT[:, d, NP_:N], tmp, xT[:, d, NP_:N], ALU.add)

            dve.wait_ge(S("ident_made"), 1)

            def step(s, i, base):
                n, m, a = POS[i]
                k = s[0]
                l = s[1] if len(s) > 1 else 0
                w = lambda j, n_=NU: small[:, j:j + n_]
                if k == 'start':
                    for d in range(0, KT, 2):
                        got(base, d)
                        dve.tensor_copy(xT[:, d, :], bank[d][:, 0:N]).then_inc(read[d], 1)
                elif k == 'params':
                    got(base, 0)
                    dve.tensor_copy(pT[:, :, :], bank[0][:, 0:3 * P].rearrange("p (c j) -> p c j", c=3)).then_inc(read[0], 1)
                    got(base, 1)
                    dve.tensor_copy(PBR[:, :, :, :], bank[1][:, 0:16].rearrange("p (k l h) -> p k l h", k=2, l=2)).then_inc(read[1], 1)
                    dve.wait_ge(read[1], base[1] + 1)
                    p4 = PBR[:, :, :, :].rearrange("p k l h -> p (k l) h")
                    for c in range(2):
                        dst = par[:, :, :, 0:8].rearrange("p k l (h c) -> p (k l) h c", c=2)[:, :, :, c]
                        dve.tensor_copy(dst, p4)
                    then(dve.tensor_tensor(PTM[:, :, :], p4, rep(hm[:, :], 1, 4), ALU.mult))
                    then(dve.tensor_reduce(par[:, :, :, 8].rearrange("p k l -> p (k l)"), PTM[:, :, :], AX_X, ALU.add))
                    dve.nop().then_inc(S("par_made"), 1)
                    got(base, 2)
                    dve.tensor_copy(cT[:, :, 0:9], bank[2][:, 0:72].rearrange("p (k j) -> p k j", j=9)).then_inc(read[2], 1)
                    dve.wait_ge(S("a_exp"), 1)
                    then(dve.tensor_scalar(par[:, 1, :, :], par[:, 1, :, :], -1.0, None, ALU.mult))
                elif k == 'adaT':
                    c = s[2]
                    got(base, 5)
                    kind = c // 2
                    bias = rep(pT[:, 0, l * 48 + 4 * c:l * 48 + 4 * c + 4], 2, 9)
                    dve.scalar_tensor_tensor(mod[:, l, 4 * c:4 * c + 4, :], bank[5][:, 0:36].rearrange("p (j s) -> p j s", j=4),
                                             1.0 if kind in (1, 2, 4, 5) else 0.0, bias, ALU.add, ALU.add).then_inc(read[5], 1)
                elif k == 'u':
                    which = 2 * l + s[2]
                    dve.wait_ge(S("consts_made"), 1)
                    dve.wait_ge(read[5], base[5])
                    sh, sc = (0, 1) if s[2] == 0 else (3, 4)
                    if s[2] == 1:
                        dve.wait_ge(S("nsc_stored"), 32 * (l + 1))
                        dve.wait_ge(S("sd_stored"), 16 * (l + 1))
                        dve.wait_ge(S("sp_stored"), 16 * (l + 1))
                    if which == 0:
                        fac, add = mod[:, l, sc * KT:sc * KT + KT, :], mod[:, l, sh * KT:sh * KT + KT, :]
                    else:
                        fac, add = UAB[:, 0, :, :], UAB[:, 1, :, :]
                    v = U32[:, :, NP_:N].rearrange("p k (s t) -> p k s t", s=NSEQ)
                    xs = xT[:, :, NP_:N].rearrange("p k (s t) -> p k s t", s=NSEQ)
                    then(dve.tensor_tensor(v, xs, rep(fac[:, :, 1:], 3, NT), ALU.mult))
                    dve.tensor_tensor(v, v, rep(add[:, :, 1:], 3, NT), ALU.add)
                    for d in range(KT):
                        op = dve.tensor_scalar(U32[:, d, 0:NP_], xT[:, d, 0:NP_], fac[:, d, 0:1], add[:, d, 0:1],
                                               ALU.mult, ALU.add)
                        if d % 2 == 1:
                            op.then_inc(S("u_made"), 1)
                    for q in range(QTR):
                        dve.wait_ge(S("uh_made"), QTR * which + q + 1)
                        v = slice(2 * q, 2 * q + 2)
                        op = dve.tensor_tensor(UL[:, v, :], U32[:, v, :], UH[:, v, :].bitcast(F32), ALU.subtract)
                    op.then_inc(S("u_split"), 1)
                elif k == 'st_in':
                    if l > 0:
                        dve.wait_ge(S("u_split"), 2 * l + 1)
                    dve.memset(EXT[:, :, 0:DK - 1], 0.0)
                    then(dve.memset(CH[:, :, 0:CK - 1], 0.0))
                    got(base, 6)
                    dve.tensor_copy(EXT[:, :, DS0:].rearrange("p j (s t) -> p j s t", s=NSEQ)[:, :, :, 0:DK - 1],
                                    bank[6][:, 0:24 * QT].rearrange("p (j s t) -> p j s t", j=QT, s=NSEQ)).then_inc(S("ext_cleared"), 1)
                    dve.tensor_copy(CH[:, :, CS0:].rearrange("p j (s t) -> p j s t", s=NSEQ)[:, :, :, 0:CK - 1],
                                    bank[6][:, 24 * QT:24 * QT + 64].rearrange("p (j s t) -> p j s t", j=CT, s=NSEQ)).then_inc(read[6], 1)
                elif k == 'ba2':
                    got(base, 7)
                    dve.tensor_copy(small[:, 224:248], bank[7][:, 0:24]).then_inc(read[7], 1)
                    dve.wait_ge(read[7], base[7] + 1)
                    tk = small[:, 224:248].rearrange("p (c k h) -> p c k h", c=3, k=2)
                    for kind in range(2):
                        dve.tensor_copy(w(16 * kind, 8).rearrange("p (h c) -> p c h", c=2), tk[:, 0:2, kind, :])
                    t8 = small[:, 248:256].rearrange("p (k h) -> p k h", k=2)
                    then(dve.tensor_tensor(t8, tk[:, 2, :, :], rep(hm[:, :], 1, 2), ALU.mult))
                    then(dve.tensor_reduce(small[:, 0:32].rearrange("p (k j) -> p k j", k=2)[:, :, 8], t8, AX_X, ALU.add))
                    then(dve.tensor_tensor(w(48), w(16), par[:, 0, l, :], ALU.add))
                    then(dve.scalar_tensor_tensor(w(32), w(48), -1.0, w(48), ALU.mult, ALU.max))
                    dve.nop().then_inc(S("ab_made"), 1)
                    dve.wait_ge(S("gate_exps"), l + 1)
                    then(dve.tensor_scalar(w(96), w(96), 1.0, None, ALU.add))
                    then(dve.reciprocal(w(208), w(96)))
                    dve.wait_ge(S("gate_ln"), l + 1)
                    then(dve.scalar_tensor_tensor(w(80), w(48), 0.0, w(128), ALU.max, ALU.add))
                    then(dve.tensor_tensor(w(64), w(80), par[:, 1, l, :], ALU.mult))
                elif k in ('pt', 'wo'):
                    t = s[3]
                    b = t
                    if k == 'wo':
                        dve.wait_ge(read[5], base[5])
                        got(base, b)
                        if s[2] == 0 and t == 0:
                            dve.wait_ge(S("x_scaled"), 2 * l + 1)
                        last = add_scaled(bank[b], 2 * s[2] + t, l, 2, WTM[:, t, :])
                        last.then_inc(read[b], 1)
                        if s[2] == 3 and t == 1:
                            dve.wait_ge(read[b], base[b] + 1)
                            dve.nop().then_inc(S("x_added"), 1)
                    else:
                        what, blk_ = W_IN[s[2]]
                        if what == 'h':
                            j = (blk_ - 4) * 2 + t
                            got(base, b)
                            for x, (dst, sl) in enumerate(zip(halves(CH[:, j, :], CK - 1), (slice(0, NP_), slice(NP_, N)))):
                                in0, in1 = bank[b][:, sl], CTM[:, t, sl]
                                if x:
                                    in0 = in0.rearrange("p (s t) -> p s t", s=NSEQ)
                                    in1 = in1.rearrange("p (s t) -> p s t", s=NSEQ)
                                op = dve.tensor_tensor(dst, in0, in1, ALU.mult)
                            op.then_inc(read[b], 1)
                            if j == CT - 1:
                                dve.wait_ge(read[b], base[b] + 1)
                                dve.tensor_copy(CSC[:, :, 0:2], CH[:, :, CS0 - 2:CS0])
                                then(dve.tensor_copy(CSC[:, :, 2:18].rearrange("p j (s t) -> p j s t", s=NSEQ),
                                                     CH[:, :, CS0:].rearrange("p j (s t) -> p j s t", s=NSEQ)[:, :, :, NT:]))
                                dve.nop().then_inc(S("cs_taken"), 1)
                        elif what == 'b':
                            j = blk_ * 2 + t
                            wk = lambda q: pT[:, 1, 96 + (l * CK + q) * CT + j:97 + (l * CK + q) * CT + j]
                            W_ = CE - CK + 1
                            y = YTM[:, 0:W_]
                            then(dve.tensor_scalar(y, CH[:, j, 0:W_], wk(0), None, ALU.mult))
                            for q in (1, 2):
                                then(dve.scalar_tensor_tensor(y, CH[:, j, q:q + W_], wk(q), y, ALU.mult, ALU.add))
                            got(base, b)
                            dve.tensor_tensor(CH[:, j, 0:NP_], bank[b][:, 0:NP_], y[:, 0:NP_], ALU.mult)
                            ys = YTM[:, CS0:].rearrange("p (s t) -> p s t", s=NSEQ)[:, :, 0:NT]
                            dve.tensor_tensor(CH[:, j, NP_:N].rearrange("p (s t) -> p s t", s=NSEQ),
                                              bank[b][:, NP_:N].rearrange("p (s t) -> p s t", s=NSEQ), ys,
                                              ALU.mult).then_inc(read[b], 1)
                elif k == 'conv':
                    g = 'kqv'.index(s[2])
                    q0 = {'q': 0, 'k': H, 'v': 2 * H}[s[2]]
                    dve.wait_ge(read[1], base[1])
                    dve.wait_ge(read[0], base[0])
                    if 3 * l + g > 0:
                        dve.wait_ge(S("conv_done"), 3 * l + g)
                    W_ = DE - DK + 1
                    for h in range(H):
                        wk = lambda q: pT[:, 2, (l * DK + q) * QT + q0 + h:(l * DK + q) * QT + q0 + h + 1]
                        y = CB[:, h, 0:W_]
                        then(dve.tensor_scalar(y, EXT[:, q0 + h, 0:W_], wk(0), None, ALU.mult))
                        for q in (1, 2, 3):
                            op = dve.scalar_tensor_tensor(y, EXT[:, q0 + h, q:q + W_], wk(q), y, ALU.mult, ALU.add)
                            if q < 3:
                                then(op)
                    op.then_inc(S("conv_made"), 1)
                    if s[2] == 'v':
                        dve.tensor_copy(CST[:, :, 0:3], EXT[:, :, DS0 - 3:DS0])
                        dve.tensor_copy(CST[:, :, 3:27].rearrange("p j (s t) -> p j s t", s=NSEQ),
                                        EXT[:, :, DS0:].rearrange("p j (s t) -> p j s t", s=NSEQ)[:, :, :, NT:]).then_inc(S("past_taken"), 1)
                elif k == 'ss':
                    q0 = 0 if s[2] == 'q' else H
                    dve.wait_ge(S("norm_made"), 2 * l + 1 + (s[2] == 'q'))
                    v = QKV[:, q0:q0 + H, :]
                    if s[2] == 'k':
                        then(dve.tensor_tensor(v, v, RB[:, :, :], ALU.mult))
                        dve.tensor_copy(KV8[:, 0, :].rearrange("p (h t) -> p h t", h=H), QKV[:, H:2 * H, NP_:N]).then_inc(S("k_normed"), 1)
                    else:
                        dve.scalar_tensor_tensor(v, v, P ** -0.5, RB[:, :, :], ALU.mult, ALU.mult).then_inc(S("q_normed"), 1)
                    if s[2] == 'q':
                        dve.tensor_tensor(GU[:, 0:8, :], rep(tri[:, :], 1, 8), rep(small[:, 64:72], 2, P), ALU.mult)
                        dve.tensor_scalar(GU[:, 8, :], tri4[:, :], small[:, 72:73], None, ALU.mult).then_inc(S("g_made"), 1)
                elif k == 'gc':
                    dve.wait_ge(S("conv_done"), 3 * (l + 1))
                    dve.tensor_copy(KV8[:, 1, :].rearrange("p (h t) -> p h t", h=H), QKV[:, 2 * H:3 * H, NP_:N]).then_inc(S("v8_made"), 1)
                    got(base, 2)
                    dve.tensor_copy(w(144), bank[2][:, 0:9])
                    then(dve.tensor_copy(w(176), bank[2][:, 16:25]))
                    then(dve.tensor_tensor(w(160), w(176), w(144), ALU.subtract))
                    dve.nop().then_inc(read[2], 1)
                    dve.nop().then_inc(S("gc_made"), 1)
                    dve.wait_ge(S("eg_made"), l + 1)
                    for u in range(NU):
                        b = (3, 6, 7)[u // 4]
                        if u % 4 == 0:
                            got(base, b)
                        src = bank[b][:, (u % 4) * P:(u % 4) * P + P]
                        dve.tensor_scalar(GS[:, u, :], src, w(144 + u, 1), 0.0, ALU.subtract, ALU.max)
                        op = dve.tensor_scalar(GI[:, u, :], src, w(144 + u, 1), 0.0, ALU.subtract, ALU.min)
                    op.then_inc(S("gs_diff"), 1)
                    dve.wait_ge(S("gs_diff"), l + 1)
                    for b in (3, 6, 7):
                        dve.nop().then_inc(read[b], 1)
                    dve.wait_ge(S("decays"), l + 1)
                    dve.tensor_tensor(w(80), w(208), w(176), ALU.mult).then_inc(S("bg_made"), 1)
                    dve.wait_ge(S("gammas"), l + 1)
                    for mk, mk4, t_ in ((lows, lows4, GS), (tri, tri4, GI)):
                        dve.tensor_tensor(t_[:, 0:8, :], t_[:, 0:8, :], rep(mk[:, :], 1, 8), ALU.mult)
                        then(dve.tensor_tensor(t_[:, 8, :], t_[:, 8, :], mk4[:, :], ALU.mult))
                    for h in range(H):
                        dve.tensor_tensor(QD[:, h, :], QKV[:, h, P:NP_], EG[:, h, :], ALU.mult)
                    dve.tensor_tensor(WQ[:, 1, :].rearrange("p (h t) -> p h t", h=H), QKV[:, 0:H, NP_:N],
                                      EG[:, 4, :].rearrange("p (h t) -> p h t", h=H), ALU.mult)
                elif k == 'tok':
                    for q, b in enumerate((2, 3, 6)):
                        dve.wait_ge(S("kd_bank"), 3 * l + q + 1)
                        for x, u in enumerate([4 * q + y for y in range(4)] if q < 2 else [8]):
                            if u in C1U:
                                op = dve.tensor_scalar(R[:, C1U.index(u), :], bank[b][:, x * P:x * P + P], w(80 + u, 1), None, ALU.mult)
                        op.then_inc(read[b], 1)
                elif k == 'att':
                    for q, b in enumerate((6, 7, 2)):
                        got(base, b)
                        us = slice(4 * q, 4 * q + 4) if q < 2 else slice(8, 9)
                        w_ = (us.stop - us.start) * P
                        dve.tensor_tensor(ATT[:, us, :], bank[b][:, 0:w_].rearrange("p (u t) -> p u t", t=P), GI[:, us, :],
                                          ALU.mult).then_inc(read[b], 1)
                elif k == 'kk':
                    for u in range(NU):
                        b = (3, 6, 7)[u // 4]
                        if u == 0:
                            got(base, 7)
                        if u % 4 == 0:
                            got(base, b)
                        op = dve.scalar_tensor_tensor(M[:, u, :], bank[b][:, (u % 4) * P:(u % 4) * P + P], w(208 + u, 1),
                                                      GS[:, u, :], ALU.mult, ALU.mult)
                        if u % 4 == 3 or u == 8:
                            op.then_inc(read[b], 1)
                    dve.wait_ge(read[7], base[7] + 1)
                    dve.nop().then_inc(S("m_made"), 1)
                elif k == 'mt':
                    then(dve.tensor_tensor(Tm[:, :, :], M[:, :, :], rep(lev[1][:, :], 1, NU), ALU.mult))
                    then(dve.tensor_tensor(Tm[:, :, :], rep(ident[:, :], 1, NU), Tm[:, :, :], ALU.subtract))
                    dve.wait_ge(read[6], base[6] + 1)
                    then(dve.tensor_tensor(TTm[:, :, :], MT[:, :, :], rep(lev1T[:, :], 1, NU), ALU.mult))
                    dve.tensor_tensor(TTm[:, :, :], rep(ident[:, :], 1, NU), TTm[:, :, :], ALU.subtract).then_inc(S("t_made"), 1)
                    dve.wait_ge(S("t_made"), l + 1)
                elif k == 'X':
                    b, _, us = GRP[s[3]]
                    n_ = len(us)
                    got(base, b)
                    dve.tensor_tensor(X[:, us[0]:us[0] + n_, :], bank[b][:, 0:n_ * P].rearrange("p (u t) -> p u t", t=P),
                                      rep(lev[s[2]][:, :], 1, n_), ALU.mult).then_inc(read[b], 1)
                    dve.wait_ge(read[b], base[b] + 1)
                elif k == 'Y':
                    b, bt, us = GRP[s[3]]
                    n_ = len(us)
                    for t_, bb in ((Tm, b), (TTm, bt)):
                        if t_ is Tm and s[2] == 64:
                            continue
                        got(base, bb)
                        v = t_[:, us[0]:us[0] + n_, :]
                        dve.tensor_tensor(v, v, bank[bb][:, 0:n_ * P].rearrange("p (u t) -> p u t", t=P),
                                          ALU.subtract).then_inc(read[bb], 1)
                    dve.wait_ge(read[bt], base[bt] + 1)
                elif k == 'wt':
                    got(base, 6)
                    dve.tensor_copy(V[:, 0:8, :].rearrange("p (h c) t -> p h c t", c=2)[:, :, 0, :],
                                    bank[6][:, :].rearrange("p (h t) -> p h t", h=H)).then_inc(read[6], 1)
                elif k == 'c0':
                    got(base, 2)
                    dve.tensor_copy(SP[:, :, :], bank[2][:, :].rearrange("p (h t) -> p h t", h=H)).then_inc(read[2], 1)
                    got(base, 3)
                    dve.tensor_scalar(WQ[:, 0, :], bank[3][:, 0:P], -1.0, None, ALU.mult)
                    dve.tensor_copy(WQ[:, 1, :], bank[3][:, P:2 * P]).then_inc(read[3], 1)
                elif k == 'c1':
                    got(base, 6)
                    dve.tensor_copy(V[:, 0:8, :].rearrange("p (h c) t -> p h c t", c=2)[:, :, 1, :],
                                    bank[6][:, :].rearrange("p (h t) -> p h t", h=H)).then_inc(read[6], 1)
                    got(base, 3)
                    dve.tensor_copy(V[:, DEC, :], bank[3][:, 0:P]).then_inc(read[3], 1)
                    dve.wait_ge(read[3], base[3] + 1)
                    dve.tensor_tensor(VX[:, :, :], rep(V[:, DEC, :], 1, NSEQ), rep(mask8[:, :], 2, P),
                                      ALU.mult).then_inc(S("vx_made"), 1)
                elif k == 'c2':
                    got(base, 3)
                    dve.tensor_tensor(OT[:, :, NP_:N], bank[3][:, 0:P].rearrange("p (h t) -> p h t", h=H),
                                      WQ[:, 1, :].rearrange("p (h t) -> p h t", h=H), ALU.add).then_inc(S("o_dec"), 1)
                    dve.nop().then_inc(read[3], 1)
                    got(base, 7)
                    got(base, 2)
                    for h in range(H):
                        op = dve.scalar_tensor_tensor(SP[:, h, :], SP[:, h, :], EG[:, h, P - 1:P],
                                                      bank[2][:, h * P:h * P + P], ALU.mult, ALU.add)
                    op.then_inc(read[2], 1)
                    dve.wait_ge(read[2], base[2] + 1)
                    dve.nop().then_inc(S("s2_made"), 1)
                elif k == 'su':
                    h = s[2]
                    dec = EG[:, 4, h * NS:h * NS + NS].rearrange("p (s t) -> p s t", t=NT)[:, :, NT - 1]
                    then(dve.tensor_tensor(SD[:, :, h, :], SD[:, :, h, :], rep(dec, 2, P), ALU.mult))
                    for q, b in enumerate((2, 3) if h % 2 == 0 else (6, 7)):
                        got(base, b)
                        v = SD[:, 4 * q:4 * q + 4, h, :]
                        dve.tensor_tensor(v, v, bank[b][:, :].rearrange("p (s t) -> p s t", t=P), ALU.add).then_inc(read[b], 1)
                    if h == H - 1:
                        dve.wait_ge(read[7], base[7] + 1)
                        dve.nop().then_inc(S("sd_made"), 1)
                elif k == 'on':
                    nw = pT[:, 1, 64 + l:65 + l]
                    for b in (0, 1):
                        dve.wait_ge(read[b], base[b])
                    dve.wait_ge(S("o_norm"), l + 1)
                    then(dve.scalar_tensor_tensor(OT[:, :, :], OT[:, :, :], nw, RBO[:, :, :], ALU.mult, ALU.mult))
                    then(dve.tensor_tensor(OT[:, :, :], OT[:, :, :], Z[:, :, :], ALU.mult))
                    dve.nop().then_inc(S("o_gated"), 1)
                elif k == 'mix':
                    dve.nop().then_inc(S("y_made"), 1)
                    dve.wait_ge(S("mixed_hi"), l + 1)
                    dve.tensor_tensor(UL[:, 0:CT, :], CH[:, :, 0:N], UH[:, 0:CT, :].bitcast(F32), ALU.subtract)
                    dve.tensor_tensor(UL[:, CT:KT, :], OT[:, :, :], UH[:, CT:KT, :].bitcast(F32), ALU.subtract).then_inc(S("mixed"), 1)
                elif k == 'lnm':
                    got(base, 6)
                    dve.tensor_scalar(LNM[:, :], bank[6][:, 0:N], 1.0 / D, None, ALU.mult).then_inc(read[6], 1)
                    dve.wait_ge(read[6], base[6] + 1)
                    for q in range(QTR):
                        v = xT[:, 2 * q:2 * q + 2, :]
                        dve.tensor_tensor(v, v, rep(LNM[:, :], 1, 2), ALU.subtract).then_inc(S("x_centred"), 1)
                    dve.wait_ge(S("x_centred"), QTR * (2 * l + s[2] + 1))
                elif k == 'lnv':
                    which = 2 * l + s[2]
                    o_ = which * KT
                    g_, b_ = pT[:, 1, o_:o_ + KT], pT[:, 1, 32 + o_:32 + o_ + KT]
                    final = which == 2 * DEPTH - 1
                    if not final:
                        dve.wait_ge(read[5], base[5])
                        l2, s2 = (which + 1) // 2, (which + 1) % 2
                        sh, sc = (3 * KT, 4 * KT) if s2 else (0, KT)
                        sc_ = mod[:, l2, sc:sc + KT, :]
                        dve.tensor_tensor(UAB[:, 0, :, :], sc_, rep(g_, 2, 1 + NSEQ), ALU.mult)
                        then(dve.tensor_tensor(UAB[:, 1, :, :], sc_, rep(b_, 2, 1 + NSEQ), ALU.mult))
                        dve.tensor_tensor(UAB[:, 1, :, :], UAB[:, 1, :, :], mod[:, l2, sh:sh + KT, :], ALU.add)
                        dve.tensor_scalar(XAB[:, 0, :], g_, ALPHA, None, ALU.mult)
                        dve.tensor_scalar(XAB[:, 1, :], b_, ALPHA, None, ALU.mult)
                    dve.wait_ge(S("ln_rstd"), which + 1)
                    for q in range(QTR):
                        v = xT[:, 2 * q:2 * q + 2, :]
                        op = dve.tensor_tensor(v, v, rep(LNR[:, :], 1, 2), ALU.mult)
                    then(op)
                    if final:
                        for d in range(KT):
                            op = dve.tensor_scalar(xT[:, d, :], xT[:, d, :], g_[:, d:d + 1], b_[:, d:d + 1], ALU.mult, ALU.add)
                            if d % 4 == 3:
                                op.then_inc(S("x_normed"), 1)
                elif k == 'ffn':
                    def low(r, b):
                        s_ = (m + b) % SPLIT
                        cols = BLK if b < 2 * UP_CB else DOWN_K[(b - 2 * UP_CB) % 3] * 256
                        dve.wait_ge(S("hi_made"), r * 6 + (m + b + 1))
                        dve.tensor_tensor(lo[s_][:, 0:cols], raw[:, (n + b) % RAW, 0:cols],
                                          hi[s_][:, 0:cols].bitcast(F32), ALU.subtract).then_inc(S("lo_made_dve"), 1)

                    def finish(r, c):
                        j = r * 3 + c
                        low(r, 2 * c + 2)
                        dve.wait_ge(S("ffn_mm"), r * 6 + (2 * c + 2))
                        dve.wait_ge(S("ffn_gate_read"), j + 1)
                        if not isinstance(j, int) or j > 0:
                            dve.wait_ge(S("h_split"), j)
                        for t in range(2):
                            op = dve.tensor_tensor(HF[:, t, :], SG[:, t, :], bank[2 + t][:, 0:N], ALU.mult)
                        op.then_inc(S("ffn_up_read"), 1)
                        dve.wait_ge(S("ffn_up_read"), j + 1)
                        dve.nop().then_inc(S("hf_made"), 1)
                        low(r, 2 * c + 3)
                        dve.wait_ge(S("hh_made"), j + 1)
                        dve.tensor_tensor(HL[:, bass.ds(j * 2, 2), :], HF[:, :, :], HH[:, bass.ds(j * 2, 2), :].bitcast(F32),
                                          ALU.subtract).then_inc(S("h_split"), 1)
                    for c in range(2):
                        dve.nop().then_inc(S(f"down_read{c}"), 1)
                    low(0, 0)
                    low(0, 1)
                    for c in range(3):
                        finish(0, c)
                    with dve.Fori(1, UP_ROUNDS) as r:
                        for c in range(3):
                            finish(r, c)
                    for c in range(3 * UP_ROUNDS, UP_CB):
                        finish(0, c)
                    for cb in range(4):
                        for b in range(2 * UP_CB + 3 * cb + 1, min(2 * UP_CB + 3 * cb + 4, FFN_BLOCKS)):
                            if b > 2 * UP_CB + 1:
                                low(0, b)
                        dve.wait_ge(S("ffn_mm"), 2 * UP_CB + 3 * cb + 3)
                        for t in range(2):
                            last = add_scaled(bank[4 * (cb % 2) + t], 2 * cb + t, l, 5, WTM2[:, t, :])
                        last.then_inc(S(f"down_read{cb % 2}"), 1)
                    dve.wait_ge(S("down_read1"), 3)
                    dve.nop().then_inc(S("x_added"), 1)
                elif k == 'moe':
                    x_lo(dve, 1, 0, "lo_made_dve")
                    for j in range(NE):
                        dve.memset(IDX[:, j:j + 1], float(NE - j))
                    dve.memset(YACC[:, :, :], 0.0).then_inc(S("y_added"), 1)
                    dve.wait_ge(S("logits_turned"), 1)
                    lg = bank[7][0:TT, 0:NTT * NE].rearrange("p (c j) -> p c j", c=NTT)
                    then(dve.tensor_reduce(RED[:, :], lg, AX_X, ALU.max))
                    dve.tensor_tensor(PR[:, :, :], lg, rep(RED[:, :], 2, NE), ALU.subtract).then_inc(S("logits_shifted"), 1)
                    dve.wait_ge(S("router_exp"), 1)
                    dve.nop().then_inc(S("router_read"), 1)
                    then(dve.tensor_reduce(RED[:, :], PR[:, :, :], AX_X, ALU.add))
                    then(dve.reciprocal(RED[:, :], RED[:, :]))
                    then(dve.tensor_tensor(PR[:, :, :], PR[:, :, :], rep(RED[:, :], 2, NE), ALU.mult))
                    for which, src, dst in ((0, PR, SEL), (1, SE2, SE2)):
                        if which:
                            then(dve.scalar_tensor_tensor(SE2[:, :, :], SEL[:, :, :], -2.0, PR[:, :, :], ALU.mult, ALU.add))
                        then(dve.tensor_reduce(RED[:, :], src[:, :, :], AX_X, ALU.max))
                        then(dve.tensor_tensor(EQ[:, :, :], src[:, :, :], rep(RED[:, :], 2, NE), ALU.is_equal))
                        then(dve.tensor_tensor(EQ[:, :, :], EQ[:, :, :], rep(IDX[0:TT, :], 1, NTT), ALU.mult))
                        then(dve.tensor_reduce(RED[:, :], EQ[:, :, :], AX_X, ALU.max))
                        then(dve.tensor_tensor(dst[:, :, :], EQ[:, :, :], rep(RED[:, :], 2, NE), ALU.is_equal))
                    then(dve.tensor_tensor(SEL[:, :, :], SEL[:, :, :], SE2[:, :, :], ALU.add))
                    then(dve.tensor_tensor(PR[:, :, :], PR[:, :, :], SEL[:, :, :], ALU.mult))
                    then(dve.tensor_reduce(RED[:, :], PR[:, :, :], AX_X, ALU.add))
                    then(dve.reciprocal(RED[:, :], RED[:, :]))
                    then(dve.tensor_tensor(PR[:, :, :], PR[:, :, :], rep(RED[:, :], 2, NE), ALU.mult))
                    dve.wait_ge(S("u_split"), 2 * l + 2)
                    for c in range(NTT):
                        last = dve.tensor_tensor(DG[:, :, c, :], rep(ident[0:TT, 0:TT], 1, NE), rep(PR[:, c, :], 2, TT), ALU.mult)
                    last.then_inc(S("dg_made"), 1)

                    def expert(e, last):
                        for b in range(XB):
                            if (b + 3) % 2 == 1 and not (last and b + 3 >= XB):
                                x_lo(dve, b + 3, e, "lo_made_dve")
                            j = b // 2
                            n_t = x_cols(b)[1] // P
                            if b < XUP and b % 2 == 1:
                                dve.wait_ge(S("x_mm"), e * XB + (b + 1))
                                dve.wait_ge(S("x_gate_read"), e * XCB + (j + 1))
                                if j == 0:
                                    dve.wait_ge(S("y_added"), e * XDB + 1)
                                else:
                                    dve.wait_ge(S("xh_split"), e * XCB + j)
                                for t in range(n_t):
                                    op = dve.tensor_tensor(XHF[:, t, :], XSG[:, t, :], bank[2 + t][:, 0:N], ALU.mult)
                                op.then_inc(S("x_up_read"), 1)
                                dve.wait_ge(S("x_up_read"), e * XCB + (j + 1))
                                dve.nop().then_inc(S("xhf_made"), 1)
                                dve.wait_ge(S("xhh_made"), e * XCB + (j + 1))
                                dve.tensor_tensor(XHL[:, 2 * j:2 * j + n_t, :], XHF[:, 0:n_t, :],
                                                  XHH[:, 2 * j:2 * j + n_t, :].bitcast(F32), ALU.subtract).then_inc(S("xh_split"), 1)
                            elif b >= XUP and b % 2 == 1:
                                cb = (b - XUP) // 2
                                dve.wait_ge(S("x_mm"), e * XB + (b + 1))
                                dve.wait_ge(S("gb_made"), e + 1)
                                dve.wait_ge(S("y_added"), e * XDB + (cb + 1))
                                for t in range(2):
                                    op = dve.tensor_tensor(XHF[:, t, :], bank[4 + 2 * (cb % 2) + t][:, 0:N], GB[:, :], ALU.mult)
                                op.then_inc(S("y_scaled"), 1)
                                dve.wait_ge(S("y_scaled"), e * XDB + (cb + 1))
                                v = YACC[:, 2 * cb:2 * cb + 2, :]
                                dve.tensor_tensor(v, v, XHF[:, :, :], ALU.add).then_inc(S("y_added"), 1)
                                if last:
                                    dve.wait_ge(S("y_added"), (NE - 1) * XDB + cb + 2)
                                    for d in (2 * cb, 2 * cb + 1):
                                        op = add_scaled(YACC[:, d, :], d, l, 5, YTM2[:, d % 2, :])
                                    then(op)
                    with dve.Fori(0, NE - 1) as e:
                        expert(e, False)
                    expert(NE - 1, True)
                    dve.nop().then_inc(S("x_added"), 1)

            walk(step)


_INS = ['x_prompt', 'x_sample', 'state_conv', 'state_dn_conv', 'state_dn', 'c_prompt', 'c_sample',
        'w_in', 'conv_w', 'dn_conv_w', 'a_log', 'dt_bias', 'dn_norm_w', 'w_out', 'w_ada', 'b_ada', 'ln_g', 'ln_b',
        'w_ff_gate', 'w_ff_up', 'w_ff_down', 'w_router', 'b_router', 'w_exp_gate', 'w_exp_up', 'w_exp_down']
_OUTS = [(1, NP_, D), (NSEQ, NT, D), (DEPTH, 1, CK - 1, CW), (DEPTH, 1, DK - 1, QT * P), (DEPTH, 1, H, P, P),
         (DEPTH, NSEQ, CK - 1, CW), (DEPTH, NSEQ, DK - 1, QT * P), (DEPTH, NSEQ, H, P, P)]


def kernel(**inputs):
    import numpy as _np
    import concourse.bacc as _bacc
    from concourse import mybir as _mybir
    from concourse.bass_utils import run_bass_kernel_spmd as _run

    nc = _bacc.Bacc("TRN2", target_bir_lowering=False, num_devices=1)
    arrays, ins, outs = {}, {}, []
    for name in _INS:
        a = _np.ascontiguousarray(inputs[name])
        arrays[f"in_{name}_dram"] = a
        ins[name] = nc.dram_tensor(f"in_{name}_dram", a.shape, _mybir.dt.from_np(a.dtype), kind="ExternalInput").ap()
    for i, shape in enumerate(_OUTS):
        outs.append(nc.dram_tensor(f"out_{i}_dram", shape, _mybir.dt.float32, kind="ExternalOutput").ap())
    program(nc, ins, outs)
    r = _run(nc, [arrays], core_ids=[0])
    return tuple(r.results[0][f"out_{i}_dram"] for i in range(len(_OUTS)))
```
